# Optimizing a Trainium2 kernel written in Bass

```python
import math
import jax, jax.numpy as jnp
from jax import lax
import numpy as np

D_MODEL = 2048
BATCH = 1
SEQ = 256
DEPTH = 2

N_A = (DEPTH + 1) // 2
N_B = DEPTH - N_A

D_RNN = D_MODEL
LRU_BLOCK = 256
N_BLK = D_RNN // LRU_BLOCK
CONV_W = 4
LRU_C = 8.0

N_HEADS = D_MODEL // 128
NOPE_D = 128
ROPE_D = 64
QK_D = NOPE_D + ROPE_D
V_D = 128
Q_LORA = 512
KV_LORA = 512
ROPE_THETA = 10000.0
Q_BLOCK = 128

D_FF = ((8 * D_MODEL // 3 + 255) // 256) * 256

NORM_EPS = 1e-6

kernel_name = "yoco_rglru_mla_hybrid"

def rmsnorm(x, g):
    xf = x.astype(jnp.float32)
    y = xf * lax.rsqrt(jnp.mean(xf * xf, axis=-1, keepdims=True) + NORM_EPS)
    return (y * g.astype(jnp.float32)).astype(x.dtype)

def rope_tables(positions):
    inv_freq = ROPE_THETA ** (-jnp.arange(0, ROPE_D, 2, dtype=jnp.float32) / ROPE_D)
    ang = positions.astype(jnp.float32)[..., None] * inv_freq
    return jnp.cos(ang)[:, :, None, :], jnp.sin(ang)[:, :, None, :]

def apply_rope(t, cos, sin):
    cos = cos.astype(t.dtype)
    sin = sin.astype(t.dtype)
    t1, t2 = t[..., : ROPE_D // 2], t[..., ROPE_D // 2:]
    return jnp.concatenate([t1 * cos - t2 * sin, t2 * cos + t1 * sin], axis=-1)

def qk_finish(t, g, cos, sin):
    t = rmsnorm(t, g)
    return jnp.concatenate([t[..., :NOPE_D], apply_rope(t[..., NOPE_D:], cos, sin)], axis=-1)

def causal_conv(x, w, b):
    y = lax.conv_general_dilated(
        x, w[:, None, :].astype(x.dtype), window_strides=(1,), padding=[(CONV_W - 1, 0)],
        dimension_numbers=("NWC", "WIO", "NWC"), feature_group_count=x.shape[-1])
    return y + b

def rglru(x, w_gate, b_gate, lam):
    bsz, seq, _ = x.shape
    xb = x.reshape(bsz, seq, N_BLK, LRU_BLOCK)
    g = jnp.einsum("bsnd,nde->bsne", xb, w_gate) + b_gate
    g = jax.nn.sigmoid(g.astype(jnp.float32))
    r = g[..., :LRU_BLOCK].reshape(bsz, seq, D_RNN)
    i = g[..., LRU_BLOCK:].reshape(bsz, seq, D_RNN)
    log_a = -LRU_C * r * jax.nn.softplus(-lam.astype(jnp.float32))
    a = jnp.exp(log_a)
    mult = jnp.sqrt(-jnp.expm1(2.0 * log_a))
    bterm = mult * (i * x.astype(jnp.float32))

    def combine(left, right):
        a1, b1 = left
        a2, b2 = right
        return a1 * a2, a2 * b1 + b2

    _, h = lax.associative_scan(combine, (a, bterm), axis=1)
    return h.astype(x.dtype)

def rglru_block(hn, w_in, b_in, conv_w, conv_b, w_gate, b_gate, lam, w_out, b_out):
    u = hn @ w_in + b_in
    gate_br = u[..., :D_RNN]
    rec = causal_conv(u[..., D_RNN:], conv_w, conv_b)
    rec = rglru(rec, w_gate, b_gate, lam)
    return (jax.nn.gelu(gate_br) * rec) @ w_out + b_out

def shared_kv(h, kv_norm_in, w_dkv, kv_latent_norm, w_ukv, k_norm, cos, sin):
    bsz, seq, _ = h.shape
    hn = rmsnorm(h, kv_norm_in)
    ckr = hn @ w_dkv
    c_kv = rmsnorm(ckr[..., :KV_LORA], kv_latent_norm)
    k_rope = ckr[..., KV_LORA:]
    kv = jnp.einsum("bsc,chd->bshd", c_kv, w_ukv)
    k_nope, v = kv[..., :NOPE_D], kv[..., NOPE_D:]
    k = jnp.concatenate(
        [k_nope, jnp.broadcast_to(k_rope[:, :, None, :], (bsz, seq, N_HEADS, ROPE_D))], axis=-1)
    k = qk_finish(k, k_norm, cos, sin)
    return k.transpose(0, 2, 1, 3), v.transpose(0, 2, 1, 3)

def causal_attention(q, k, v):
    bsz, nh, seq, dk = q.shape
    n_blk = seq // Q_BLOCK
    scale = 1.0 / math.sqrt(QK_D)
    qb = q.reshape(bsz, nh, n_blk, Q_BLOCK, dk).transpose(2, 0, 1, 3, 4)
    key_idx = jnp.arange(seq)

    def one_block(args):
        q_blk, bi = args
        s = jnp.einsum("bhqd,bhkd->bhqk", q_blk, k).astype(jnp.float32) * scale
        q_idx = bi * Q_BLOCK + jnp.arange(Q_BLOCK)
        mask = key_idx[None, :] <= q_idx[:, None]
        p = jax.nn.softmax(jnp.where(mask, s, -jnp.inf), axis=-1)
        return jnp.einsum("bhqk,bhkd->bhqd", p.astype(v.dtype), v)

    out = lax.map(one_block, (qb, jnp.arange(n_blk)))
    return out.transpose(1, 0, 3, 2, 4).reshape(bsz, seq, nh, v.shape[-1])

def mla_block(hn, k_sh, v_sh, cos, sin, w_dq, q_latent_norm, w_uq, q_norm, w_o):
    bsz, seq, _ = hn.shape
    cq = rmsnorm(hn @ w_dq, q_latent_norm)
    q = jnp.einsum("bsc,chd->bshd", cq, w_uq)
    q = qk_finish(q, q_norm, cos, sin).transpose(0, 2, 1, 3)
    o = causal_attention(q, k_sh, v_sh)
    return o.reshape(bsz, seq, N_HEADS * V_D) @ w_o

def swiglu(hn, w_in, w_out):
    u = hn @ w_in
    return (jax.nn.silu(u[..., :D_FF]) * u[..., D_FF:]) @ w_out

def setup_inputs(seed: int = 0) -> dict:
    key = jax.random.key(seed)
    ks = jax.random.split(key, 32)
    f32 = jnp.float32

    def w(k, shape, fan_in):
        return jax.random.normal(k, shape, f32) * (fan_in ** -0.5)

    def gain(k, shape):
        return 1.0 + 0.02 * jax.random.normal(k, shape, f32)

    def bias(k, shape):
        return 0.02 * jax.random.normal(k, shape, f32)

    x = jax.random.normal(ks[0], (BATCH, SEQ, D_MODEL), f32)
    offset = jax.random.randint(ks[1], (BATCH, 1), 0, 1024, dtype=jnp.int32)
    positions = offset + jnp.arange(SEQ, dtype=jnp.int32)[None, :]

    u = jax.random.uniform(ks[2], (N_A, D_RNN), f32, minval=0.9, maxval=0.999)
    a0 = u ** (1.0 / LRU_C)
    lru_lambda = jnp.log(a0) - jnp.log1p(-a0)

    return {
        "x": x,
        "positions": positions,
        "norm_mix": gain(ks[3], (DEPTH, D_MODEL)),
        "norm_ffn": gain(ks[4], (DEPTH, D_MODEL)),
        "lru_w_in": w(ks[5], (N_A, D_MODEL, 2 * D_RNN), D_MODEL),
        "lru_b_in": bias(ks[6], (N_A, 2 * D_RNN)),
        "lru_conv_w": w(ks[7], (N_A, CONV_W, D_RNN), CONV_W),
        "lru_conv_b": bias(ks[8], (N_A, D_RNN)),
        "lru_w_gate": w(ks[9], (N_A, N_BLK, LRU_BLOCK, 2 * LRU_BLOCK), LRU_BLOCK),
        "lru_b_gate": bias(ks[10], (N_A, N_BLK, 2 * LRU_BLOCK)),
        "lru_lambda": lru_lambda,
        "lru_w_out": w(ks[11], (N_A, D_RNN, D_MODEL), D_RNN),
        "lru_b_out": bias(ks[12], (N_A, D_MODEL)),
        "kv_norm_in": gain(ks[13], (D_MODEL,)),
        "w_dkv": w(ks[14], (D_MODEL, KV_LORA + ROPE_D), D_MODEL),
        "kv_latent_norm": gain(ks[15], (KV_LORA,)),
        "w_ukv": w(ks[16], (KV_LORA, N_HEADS, NOPE_D + V_D), KV_LORA),
        "k_norm": gain(ks[17], (QK_D,)),
        "w_dq": w(ks[18], (N_B, D_MODEL, Q_LORA), D_MODEL),
        "q_latent_norm": gain(ks[19], (N_B, Q_LORA)),
        "w_uq": w(ks[20], (N_B, Q_LORA, N_HEADS, QK_D), Q_LORA),
        "q_norm": gain(ks[21], (N_B, QK_D)),
        "w_o": w(ks[22], (N_B, N_HEADS * V_D, D_MODEL), N_HEADS * V_D),
        "ffn_w_in": w(ks[23], (DEPTH, D_MODEL, 2 * D_FF), D_MODEL),
        "ffn_w_out": w(ks[24], (DEPTH, D_FF, D_MODEL), D_FF),
    }

def reference(x, positions, norm_mix, norm_ffn, lru_w_in, lru_b_in, lru_conv_w, lru_conv_b,
              lru_w_gate, lru_b_gate, lru_lambda, lru_w_out, lru_b_out, kv_norm_in, w_dkv,
              kv_latent_norm, w_ukv, k_norm, w_dq, q_latent_norm, w_uq, q_norm, w_o,
              ffn_w_in, ffn_w_out):
    cos, sin = rope_tables(positions)
    h = x
    k_sh = None
    v_sh = None
    for layer in range(DEPTH):
        hn = rmsnorm(h, norm_mix[layer])
        if layer < N_A:
            h = h + rglru_block(hn, lru_w_in[layer], lru_b_in[layer], lru_conv_w[layer],
                                lru_conv_b[layer], lru_w_gate[layer], lru_b_gate[layer],
                                lru_lambda[layer], lru_w_out[layer], lru_b_out[layer])
        else:
            j = layer - N_A
            h = h + mla_block(hn, k_sh, v_sh, cos, sin, w_dq[j], q_latent_norm[j], w_uq[j],
                              q_norm[j], w_o[j])
        h = h + swiglu(rmsnorm(h, norm_ffn[layer]), ffn_w_in[layer], ffn_w_out[layer])
        if layer == N_A - 1:
            k_sh, v_sh = shared_kv(h, kv_norm_in, w_dkv, kv_latent_norm, w_ukv, k_norm, cos, sin)
    return h


_drawn_inputs = setup_inputs


def setup_inputs(seed=0):
    import zlib

    import numpy as np

    out = dict(_drawn_inputs(seed))
    spreads = {}
    factors = {'norm_mix': 4.633,
     'norm_ffn': 2.833,
     'lru_b_gate': 8.0,
     'kv_norm_in': 8.0,
     'kv_latent_norm': 8.0,
     'k_norm': 8.0,
     'q_latent_norm': 8.0,
     'q_norm': 8.0,
     'lru_b_out': 2.974}
    for name, (base, spread) in spreads.items():
        noise = np.random.default_rng([zlib.crc32(name.encode()), seed]).standard_normal(out[name].shape)
        drawn = base * np.exp(spread * noise) if base else spread * noise
        out[name] = __import__('jax').numpy.asarray(drawn.astype(out[name].dtype))
    for name, factor in factors.items():
        out[name] = (out[name] * factor).astype(out[name].dtype)
    return out
```

```python
from contextlib import ExitStack

import numpy as np

import concourse.bass as bass
from concourse import mybir

F32 = mybir.dt.float32
F32R = mybir.dt.float32r
I32 = mybir.dt.int32
ALU = mybir.AluOpType
ACT = mybir.ActivationFunctionType
AX = mybir.AxisListType

P = 128
SEQ = 256
NT = SEQ // P
D = 2048
KT = D // P
FF = 5632
W = 512
KC = 4
FB = FF // W
NB = D // W
HEADS, NOPE, ROPE, QK, VD = 16, 128, 64, 192, 128
PAIRS = HEADS // 2
KV_LORA = Q_LORA = 512
DKV = KV_LORA + ROPE
HALF = DKV // 2
LT = KV_LORA // P
EPS = 1e-6
SCALE = 1.0 / float(np.sqrt(QK))
NEG = -1e30

C_REC = 0
C_GATE = C_REC + 16
C_GEL = C_GATE + 4
C_LOUT = C_GEL + 16
C_UP0 = C_LOUT + 16
C_DOWN0 = C_UP0 + 8 * FB
C_DKV = C_DOWN0 + 4 * FB
C_DQ = C_DKV + 8
C_PAIR = C_DQ + 4
C_WO = C_PAIR + 2 * PAIRS
C_UP1 = C_WO + 16
C_DOWN1 = C_UP1 + 8 * FB
CHUNKS = C_DOWN1 + 4 * FB

DOWN_C = (C_LOUT, C_DOWN0, C_WO, C_DOWN1)
DOWN_G = (4, FB, 4, FB)
DOWN_G0 = (0, 4, 4 + FB, 8 + FB)
HI0 = {"x": 0, "lru": 16, 0: 80, 1: 96, "mix": 112, 2: 128}
LO0 = {"x": 0, 0: 16, 1: 32, "mix": 48, 2: 64}

G_MIX0, G_FFN0, G_KV, G_MIX1, G_FFN1, G_CKV, G_CQ, G_KN, G_QN = 0, 16, 32, 48, 64, 80, 84, 88, 89
ROWS_A = 90
B_IN, CONV_W, CONV_B = 0, 32, 96
ROWS_B = 112
B_GATE, LAM = 0, 32
ROWS_C = 48


def act_slot(g):
    return 4 * g if g < 2 else 8 + 4 * (g % 2)


TWO_PI = (6.28125, float(np.floor((2 * np.pi - 6.28125) * 2 ** 20) / 2 ** 20))
TWO_PI += (float(2 * np.pi - sum(TWO_PI)),)
PI_DOWN = 3.1415925


def build_program(nc, a, out):
    x, positions = a["x"], a["positions"]
    ctx = ExitStack()
    with ctx:
        def sb(name, shape, dt=F32, stack=ctx):
            return stack.enter_context(nc.sbuf_tensor(name, shape, dt))

        def sem(name):
            return ctx.enter_context(nc.semaphore(name))

        h = sb("h", [P, NT, D])
        act_hi = sb("act_hi", [P, KT, SEQ], F32R)
        act_lo = sb("act_lo", [P, KT, SEQ], F32R)
        raw = sb("raw", [P, 4, KC, W])
        w_hi = sb("w_hi", [P, 4, KC, W], F32R)
        w_lo = sb("w_lo", [P, 4, KC, W], F32R)
        gtmp = sb("gtmp", [P, NT, W])
        utmp = sb("utmp", [P, 4, 260])
        ident = sb("ident", [P, P])
        mask = sb("mask", [P, 3 * P])
        cols = sb("cols", [P, 3, P])
        neg_bg = sb("neg_bg", [P, 32])
        decay = sb("decay", [P, 2, KT])
        stats = sb("stats", [P, 80])
        minus_half = sb("minus_half", [P, 8])
        rope_c = sb("rope_c", [P, 2, NT, ROPE])
        rope_s = sb("rope_s", [P, 2, NT, ROPE])
        with nc.sbuf_tensor("feat", [P, 4 * FB, SEQ], F32) as feat:
            pass
        with ExitStack() as over:
            sb("feat_0_27", [P, 28, SEQ], F32, over)
            rec_split = sb("rec_split", [P, 4, 2, 2, SEQ], F32R, over)
        with ExitStack() as over:
            sb("feat_0_15", [P, 16, SEQ], F32, over)
            v_sb = sb("v_sb", [P, 2, NT, 2, VD], F32, over)
            kn = sb("kn", [P, NT, 2, NOPE], F32, over)
            kr = sb("kr", [P, NT, 2, ROPE], F32, over)
            qn = sb("qn", [P, NT, 2, QK], F32, over)
            qr = sb("qr", [P, NT, 2, ROPE], F32, over)
            rot = sb("rot", [P, NT, 2, ROPE], F32, over)
            kr_all = sb("kr_all", [P, NT, ROPE], F32, over)
            rot_k = sb("rot_k", [P, NT, ROPE], F32, over)
            knT = sb("knT", [P, 2, SEQ], F32, over)
            qnT = sb("qnT", [P, 2, SEQ], F32, over)
            krT = sb("krT", [P, SEQ], F32, over)
            qrT = sb("qrT", [P, 2, SEQ], F32, over)
            pT = sb("pT", [P, 2, 3 * P], F32, over)
        with ExitStack() as over:
            sb("feat_0_19", [P, 20, SEQ], F32, over)
            bout = sb("bout", [P, D], F32, over)
            rows = sb("rows", [P, 3, P], F32, over)
            posi = sb("posi", [P, NT], I32, over)
            invf = sb("invf", [P, 32], F32, over)
            rope_g = sb("rope_g", [P, 2, ROPE], F32, over)
            ang = sb("ang", [P, 8, NT, 32], F32, over)
            posf = sb("posf", [P, NT], F32, over)
            sp = sb("sp", [P, 6, KT], F32, over)
        feat = sb("feat_all", [P, 4 * FB, SEQ])
        flat = feat[:, :, :].rearrange("p a b -> p (a b)")
        xn = flat[:, 0:NT * D].rearrange("p (t d) -> p t d", t=NT)
        ckr = flat[:, 0:NT * DKV].rearrange("p (t d) -> p t d", t=NT)
        cq = flat[:, 5 * SEQ:5 * SEQ + NT * Q_LORA].rearrange("p (t d) -> p t d", t=NT)
        gi = gtmp[:, :, :].rearrange("p t w -> p (t w)").rearrange("p (a b) -> p a b", a=4)
        probs = utmp[:, :, :].rearrange("p a b -> p (a b)")[:, 0:2 * 3 * P].rearrange("p (e k) -> p e k", e=2)
        sq = gtmp[:, :, :].rearrange("p t w -> p (t w)")[:, 0:NT * 2 * QK].rearrange("p (t e d) -> p t e d", t=NT, e=2)
        junk = utmp[:, :, :].rearrange("p a b -> p (a b)")[:, 0:2 * W].rearrange("p (t w) -> p t w", t=NT)
        ps = [ctx.enter_context(nc.psum_tensor(f"bank{i}", [P, W], F32)) for i in range(8)]

        SS_X, SS_D, SS_T, RS = 0, 2, 10, 12
        SS_C, RS_C, SS_Q, RS_Q, SS_KR = 20, 22, 24, 26, 28
        SS_K, RS_K, SS_QH, RS_QH = 30, 34, 38, 42
        MX, NMX, PSUMS, RPS = 46, 50, 54, 58
        SS_KR4, QK_EPS4, INV_QK4, WAIT_SLOT, POOL_SLOT = 64, 68, 72, 76, 77

        x_in = [sem(f"x_in{t}") for t in range(NT)]
        vec_in = sem("vec_in")
        bout_in = sem("bout_in")
        raw_in = [sem(f"raw_in{s}") for s in range(4)]
        w_hi_done = sem("w_hi_done")
        w_lo_done = sem("w_lo_done")
        chunk_used = sem("chunk_used")
        consts = sem("consts")
        cols_mm = sem("cols_mm")
        cols_done = sem("cols_done")
        prep = sem("prep")
        rope_done = sem("rope_done")
        x_sq = sem("x_sq")
        xn_done = sem("xn_done")
        xT_mm = sem("xT_mm")
        bout_added = sem("bout_added")
        rstd_done = sem("rstd_done")
        ms_done = sem("ms_done")
        act_hi_done = sem("act_hi_done")
        act_lo_done = sem("act_lo_done")
        conv_step = sem("conv_step")
        rec_hi = sem("rec_hi")
        rec_lo = sem("rec_lo")
        gate_half = sem("gate_half")
        sig_step = sem("sig_step")
        sig_done = sem("sig_done")
        ix_done = sem("ix_done")
        a_done = sem("a_done")
        tanh_done = sem("tanh_done")
        z_done = sem("z_done")
        conv_done = sem("conv_done")
        angles_done = sem("angles_done")
        sin_done = sem("sin_done")
        lam_done = sem("lam_done")
        lam_exp = sem("lam_exp")
        neg_bg_done = sem("neg_bg_done")
        decay_done = sem("decay_done")
        pair_step = sem("pair_step")
        q_norm = sem("q_norm")
        z_step = sem("z_step")
        sqrt_done = sem("sqrt_done")
        b_done = sem("b_done")
        scan_done = sem("scan_done")
        y_done = sem("y_done")
        st_hi = sem("st_hi")
        st_lo = sem("st_lo")
        h_done = sem("h_done")
        hT_mm = sem("hT_mm")
        hT_copied = sem("hT_copied")
        h_sq = sem("h_sq")
        silu_done = sem("silu_done")
        g_done = sem("g_done")
        gT_mm = sem("gT_mm")
        gT_act = sem("gT_act")
        gT_dve = sem("gT_dve")
        ckr_done = sem("ckr_done")
        c_sq = sem("c_sq")
        c_rstd = sem("c_rstd")
        c_norm = sem("c_norm")
        cT_mm = sem("cT_mm")
        c_hi = sem("c_hi")
        c_lo = sem("c_lo")
        cq_done = sem("cq_done")
        kr_step = sem("kr_step")
        qz_done = sem("qz_done")
        k_sq = sem("k_sq")
        k_ss = sem("k_ss")
        k_rs = sem("k_rs")
        q_sq = sem("q_sq")
        q_ss = sem("q_ss")
        q_rs = sem("q_rs")
        pool_step = sem("pool_step")
        k_norm = sem("k_norm")
        q_step = sem("q_step")
        t_mm = sem("t_mm")
        t_act = sem("t_act")
        t_dve = sem("t_dve")
        s_mm = sem("s_mm")
        s_max = sem("s_max")
        s_step = sem("s_step")
        s_exp = sem("s_exp")
        p_done = sem("p_done")
        pt_mm = sem("pt_mm")
        pt_act = sem("pt_act")
        pt_dve = sem("pt_dve")
        v_done = sem("v_done")
        o_mm = sem("o_mm")
        o_done = sem("o_done")
        stored = sem("stored")

        block = ctx.enter_context(nc.Block())

        @block.sync
        def _(sp_):
            for t in range(NT):
                sp_.dma_start(h[:, t, :], x[0, t * P:(t + 1) * P, :]).then_inc(x_in[t], 16)

            def load(m, s, src, dst=None):
                if not (isinstance(m, int) and m == 0):
                    sp_.wait_ge(w_lo_done, 4 * m + s - 3)
                sp_.dma_start(raw[:, s, :, :] if dst is None else dst, src).then_inc(raw_in[s], 16)

            def tile_rows(w, r, c, width=W):
                return w[r:r + KC * P, :].rearrange("(k p) n -> p k n", p=P)[:, :, bass.ds(c, width)]

            w_in = a["lru_w_in"][0]
            for s in range(4):
                load(0, s, tile_rows(w_in, s * KC * P, D))
            with sp_.Fori(1, NB) as j:
                for s in range(4):
                    load(j + C_REC // 4, s, tile_rows(w_in, s * KC * P, j * W + D))
            gate_rows = a["lru_w_gate"][0].rearrange("n d e -> (n d) e")
            for s in range(4):
                load(C_GATE // 4, s, tile_rows(gate_rows, s * KC * P, 0))
            with sp_.Fori(0, NB) as j:
                for s in range(4):
                    load(j + C_GEL // 4, s, tile_rows(w_in, s * KC * P, j * W))

            def down(w, c0, groups):
                by_group = w.rearrange("(g k p) n -> p g k n", k=KC, p=P)
                with sp_.Fori(0, groups) as g:
                    for b in range(NB):
                        src = by_group[:, bass.ds(g, 1), :, b * W:(b + 1) * W]
                        load(g + c0 // 4, b, src.rearrange("p g k n -> p (g k) n"))

            def up(w, c0):
                with sp_.Fori(0, FB) as i:
                    for c in range(8):
                        col = i * W + (c // 4) * FF
                        load(2 * i + (c0 // 4 + c // 4), c % 4, tile_rows(w, (c % 4) * KC * P, col))

            down(a["lru_w_out"][0], C_LOUT, 4)
            up(a["ffn_w_in"][0], C_UP0)
            down(a["ffn_w_out"][0], C_DOWN0, FB)
            for j in range(8):
                src = a["w_dkv"][2 * j * P:(2 * j + 2) * P, :].rearrange("(k p) n -> p k n", p=P)
                dst = raw[:, j % 4, :, :].rearrange("p k n -> p (k n)")[:, 0:2 * DKV]
                load((C_DKV + j) // 4, j % 4, src, dst.rearrange("p (k n) -> p k n", k=2))
            for s in range(4):
                load(C_DQ // 4, s, tile_rows(a["w_dq"][0], s * KC * P, 0))
            w_ukv = a["w_ukv"].rearrange("c h d -> c (h d)")
            w_uq = a["w_uq"][0].rearrange("c h d -> c (h d)")
            with sp_.Fori(0, PAIRS // 2) as i:
                for u in range(2):
                    load(i + C_PAIR // 4, 2 * u, tile_rows(w_ukv, 0, i * (2 * W) + u * W))
                    dst = raw[:, 2 * u + 1, :, :].rearrange("p k n -> p (k n)")[:, 0:KC * 2 * QK]
                    load(i + C_PAIR // 4, 2 * u + 1, tile_rows(w_uq, 0, i * (4 * QK) + u * 2 * QK, 2 * QK),
                         dst.rearrange("p (k n) -> p k n", k=KC))
            down(a["w_o"][0], C_WO, 4)
            up(a["ffn_w_in"][1], C_UP1)
            down(a["ffn_w_out"][1], C_DOWN1, FB)
            out_v = out[0].rearrange("(t p) d -> p t d", p=P)
            for b in range(NB):
                sp_.wait_ge(h_done, 3 * NB + b + 1)
                sp_.dma_start(out_v[:, :, b * W:(b + 1) * W], h[:, :, b * W:(b + 1) * W]).then_inc(stored, 16)
            sp_.wait_ge(stored, 16 * NB)

        def vector_loads():
            yield rows[0:16, 0, :], a["norm_mix"][0].rearrange("(r c) -> r c", c=P)
            yield rows[16:32, 0, :], a["norm_ffn"][0].rearrange("(r c) -> r c", c=P)
            yield rows[32:48, 0, :], a["kv_norm_in"].rearrange("(r c) -> r c", c=P)
            yield rows[48:64, 0, :], a["norm_mix"][1].rearrange("(r c) -> r c", c=P)
            yield rows[64:80, 0, :], a["norm_ffn"][1].rearrange("(r c) -> r c", c=P)
            yield rows[80:84, 0, :], a["kv_latent_norm"].rearrange("(r c) -> r c", c=P)
            yield rows[84:88, 0, :], a["q_latent_norm"][0].rearrange("(r c) -> r c", c=P)
            yield rows[88:89, 0, :], a["k_norm"][0:NOPE].rearrange("(r c) -> r c", c=P)
            yield rows[89:90, 0, :], a["q_norm"][0, 0:NOPE].rearrange("(r c) -> r c", c=P)
            yield rows[0:32, 1, :], a["lru_b_in"][0].rearrange("(r c) -> r c", c=P)
            yield rows[32:96, 1, :], a["lru_conv_w"][0].rearrange("w (r c) -> (w r) c", c=P)
            yield rows[96:112, 1, :], a["lru_conv_b"][0].rearrange("(r c) -> r c", c=P)
            yield rows[0:32, 2, :], a["lru_b_gate"][0].rearrange("n (r c) -> (n r) c", c=P)
            yield rows[32:48, 2, :], a["lru_lambda"][0].rearrange("(r c) -> r c", c=P)
            yield posi[:, :], positions[0].rearrange("(t p) -> p t", p=P)
            yield invf[:, :], a["inv_freq"][0:1, :].broadcast_to([P, 32])
            yield rope_g[:, 0, :], a["k_norm"][NOPE:QK].rearrange("(o d) -> o d", o=1).broadcast_to([P, ROPE])
            yield rope_g[:, 1, :], a["q_norm"][0:1, NOPE:QK].broadcast_to([P, ROPE])

        vec_loads = list(vector_loads())
        VEC_ALL = 16 * len(vec_loads)

        def col(row_tile, c):
            return cols[:, row_tile, c:c + 1]

        def stat(c, n=1):
            return stats[:, c:c + n]

        gain = {"x": G_MIX0, 0: G_FFN0, 1: G_KV, "mix": G_MIX1, 2: G_FFN1}

        def hT_psum(b, q):
            return ps[2 * b + q // 2][:, (q % 2) * SEQ:(q % 2 + 1) * SEQ]

        def lru_bank(idx, q):
            return ps[4 * (idx % 2) + q][:, 0:SEQ]

        def latent_psum(i, q):
            return ps[6 - 2 * i + q // 2][:, (q % 2) * SEQ:(q % 2 + 1) * SEQ]

        def kv_psum(t):
            return ps[t][:, :].rearrange("p (e d) -> p e d", e=2)

        def q_psum(t):
            return ps[2 + t][:, 0:2 * QK].rearrange("p (e d) -> p e d", e=2)

        def seen(t):
            return slice(0, P) if t == 0 else slice(P, 3 * P)

        def score_psum(e, t):
            return ps[4 + e][:, seen(t)]

        def prob(e, t):
            return probs[:, e, seen(t)]

        def mask_of(t):
            return mask[:, 0:P] if t == 0 else mask[:, P:3 * P]

        def gate_block_done(eng, n):
            if n % 2:
                eng.wait_ge(chunk_used, C_GATE + n // 2 + 1)
            else:
                eng.wait_ge(gate_half, n // 2 + 1)

        def source_ready(eng, d, g):
            if d == 0:
                eng.wait_ge(y_done, g + 1)
            elif d == 2:
                eng.wait_ge(o_done, 2 * g + 2)
            else:
                f0 = FB * (d // 2)
                eng.wait_ge(gT_act, g + (f0 + 1))
                eng.wait_ge(gT_dve, g + (f0 + 1))

        def chunk_size(n):
            return 2 * DKV if C_DKV <= n < C_DQ else KC * W

        def flat_chunk(buf, s, size):
            return buf[:, s, :, :].rearrange("p k n -> p (k n)")[:, 0:size]

        @block.scalar
        def _(act):
            A = nc.scalar

            def split(m, s):
                if isinstance(m, int) and 4 * m + s >= CHUNKS:
                    return
                size = chunk_size(4 * m + s) if isinstance(m, int) else KC * W
                act.wait_ge(raw_in[s], 16 * m + 16)
                if not (isinstance(m, int) and m == 0):
                    act.wait_ge(chunk_used, 4 * m + s - 3)
                A.activation(flat_chunk(w_hi, s, size), flat_chunk(raw, s, size), ACT.Copy).then_inc(w_hi_done, 1)

            def act_tiles(kind, b):
                if kind != "x":
                    act.wait_ge(hT_mm, kind * NB + b + 1)
                for q in range(4):
                    k = 4 * b + q
                    if kind == "x" and q % 2 == 0:
                        act.wait_ge(xT_mm, k // 2 + 1)
                    A.activation(act_hi[:, k, :], hT_psum(b, q), ACT.Copy,
                                 scale=col(0, gain[kind] + k)).then_inc(act_hi_done, 1)
                    if kind == 1 and q % 2:
                        A.activation(feat[:, k - 1:k + 1, :].rearrange("p a b -> p (a b)"), ps[2 * b + q // 2][:, :],
                                     ACT.Copy).then_inc(hT_copied, 1)

            def squares(d, b):
                act.wait_ge(h_done, d * NB + b + 1)
                if d + b:
                    act.wait_ge(h_sq, d * NB + b)
                for t in range(NT):
                    i = A.activation(junk[:, t, :], h[:, t, b * W:(b + 1) * W], ACT.Square,
                                     accum_out=stat(SS_D + NB * t + b))
                i.then_inc(h_sq, 1)

            def stationary(d, g, slot):
                source_ready(act, d, g)
                if not isinstance(g, int) or g >= 4:
                    act.wait_ge(chunk_used, 4 * g + (DOWN_C[d] - 4))
                elif d == 2:
                    act.wait_ge(chunk_used, DOWN_C[d])
                else:
                    act.wait_ge(chunk_used, DOWN_C[d] - 3 + g)
                A.activation(act_hi[:, slot:slot + 4, :], feat[:, bass.ds(4 * g, 4), :], ACT.Copy).then_inc(st_hi, 1)

            def gT_out(i, n):
                act.wait_ge(gT_mm, n)
                A.activation(feat[:, bass.ds(4 * i, 2), :], ps[4][:, :].rearrange("p (a b) -> p a b", a=2),
                             ACT.Copy).then_inc(gT_act, 1)

            def down(d):
                def group(g, slot_next, last=False):
                    for b in range(NB):
                        if b == 0 and isinstance(g, int) and g == 0 and d in (1, 3):
                            gT_out(FB - 1, FB * (d // 2) + FB)
                        if b == 0 and not last:
                            stationary(d, g + 1, slot_next)
                        if last and d < 3:
                            squares(d, b)
                            if b >= 1:
                                act_tiles(d, b - 1)
                        split(g + (DOWN_C[d] // 4 + 1), b)

                if DOWN_G[d] > 4:
                    group(0, act_slot(1))
                    group(1, act_slot(2))
                    with act.Fori(0, (DOWN_G[d] - 3) // 2) as i:
                        for u in range(2):
                            group(2 * i + (2 + u), act_slot(3 + u))
                else:
                    for g in range(DOWN_G[d] - 1):
                        group(g, act_slot(g + 1))
                group(DOWN_G[d] - 1, None, last=True)

            def up(f, c0, d):
                def body(i, first):
                    for c in range(8):
                        if c == 0 and first:
                            act_tiles(d, 3)
                        if c == 0 and not first:
                            gT_out(i - 1, i + FB * f)
                        if c == 3:
                            act.wait_ge(chunk_used, 8 * i + (c0 + 4))
                            if first:
                                act.wait_ge(rstd_done, d + 2)
                            for t in range(NT):
                                k = A.activation(gtmp[:, t, :], ps[t][:, :], ACT.Silu,
                                                 scale=stat(RS + 2 * (d + 1) + t))
                            k.then_inc(silu_done, 1)
                        split(2 * i + ((c0 + c + 4) // 4), c % 4)

                body(0, True)
                with act.Fori(1, FB) as i:
                    body(i, False)

            for dst, src in vec_loads:
                act.dma_start(dst, src, allow_slow_non_contiguous=True).then_inc(vec_in, 16)
            act.dma_start(bout[:, :], a["lru_b_out"][0:1, :].broadcast_to([P, D])).then_inc(bout_in, 16)
            act.wait_ge(x_in[0], 16)
            A.activation(xn[:, 0, :], h[:, 0, :], ACT.Square, accum_out=stat(SS_X)).then_inc(x_sq, 1)
            for s in range(2):
                split(0, s)
            act.wait_ge(cols_done, 3)
            for b in range(NB):
                act_tiles("x", b)
                if b == 1:
                    for s in (2, 3):
                        split(0, s)

            def rec_hi_block(n):
                act.wait_ge(conv_done, n // 2 + 1)
                if n == 0:
                    act.wait_ge(rope_done, 1)
                    act.wait_ge(decay_done, 1)
                if n >= 4:
                    gate_block_done(act, n - 4)
                A.activation(rec_split[:, n % 4, 0, :, :], feat[:, 2 * n:2 * n + 2, :], ACT.Copy).then_inc(rec_hi, 1)

            for n in range(C_REC, C_GATE):
                j = n // 4
                if n == 1:
                    act.wait_ge(lam_done, 1)
                    A.activation(sp[:, 1, :], sp[:, 0, :], ACT.Exp, scale=-1.0).then_inc(lam_exp, 1)
                if n == 4:
                    act.wait_ge(angles_done, 1)
                    A.activation(ang[:, 5, :, :], ang[:, 2, :, :], ACT.Sin)
                    A.activation(ang[:, 6, :, :], ang[:, 2, :, :], ACT.Sin, scale=-1.0)
                    A.activation(ang[:, 7, :, :], ang[:, 4, :, :], ACT.Sin).then_inc(sin_done, 1)
                if n % 4 == 3:
                    act.wait_ge(chunk_used, n + 1)
                    if j:
                        act.wait_ge(conv_done, j)
                    for q in range(4):
                        A.activation(utmp[:, q, 3:3 + SEQ], lru_bank(j, q), ACT.Identity,
                                     bias=col(1, B_IN + KT + 4 * j + q)).then_inc(act_hi_done, 1)
                if n in (7, 11):
                    rec_hi_block(n // 4 * 2 - 2)
                    rec_hi_block(n // 4 * 2 - 1)
                split((n + 4) // 4, n % 4)
            for c in range(4):
                for n in (2 * c, 2 * c + 1):
                    gate_block_done(act, n)
                    if n == 0:
                        act.wait_ge(neg_bg_done, 1)
                    if n >= 2:
                        act.wait_ge(ix_done, n - 1)
                    for q in range(4):
                        dst = feat[:, 16 + 2 * n + q, :] if q < 2 else gi[:, 2 * (n % 2) + q - 2, :]
                        A.activation(dst, lru_bank(4 + n, q), ACT.Exp, bias=neg_bg[:, 4 * n + q:4 * n + q + 1],
                                     scale=-1.0).then_inc(act_hi_done, 1)
                    if n + 4 < 8:
                        rec_hi_block(n + 4)
                split((C_GATE + c + 4) // 4, c)

            def decay_tiles(k0):
                act.wait_ge(sig_done, k0 // 2 + 2)
                if k0 == 0:
                    act.wait_ge(decay_done, 1)
                    act.wait_ge(chunk_used, C_GEL)
                if k0 >= 8:
                    act.wait_ge(scan_done, k0 - 4)
                for k in range(k0, k0 + 4):
                    A.activation(feat[:, 32 + k % 8, :], feat[:, 16 + k, :], ACT.Exp,
                                 scale=decay[:, 0, k:k + 1]).then_inc(a_done, 1)
                act.wait_ge(a_done, k0 + 4)
                for k in range(k0, k0 + 4):
                    A.activation(feat[:, 16 + k, :], feat[:, 16 + k, :], ACT.Tanh,
                                 scale=decay[:, 1, k:k + 1]).then_inc(tanh_done, 1)

            def sqrt_batch(bt):
                act.wait_ge(z_done, 2 * (bt + 1))
                s8 = feat[:, 16 + 8 * bt:24 + 8 * bt, :]
                A.activation(s8, s8, ACT.Sqrt).then_inc(sqrt_done, 1)

            for s in range(16):
                n = C_GEL + s
                if s in (0, 1, 4, 5):
                    decay_tiles({0: 0, 1: 4, 4: 8, 5: 12}[s])
                if s in (2, 6):
                    sqrt_batch(s // 4)
                if s % 4 == 3:
                    j = s // 4
                    act.wait_ge(chunk_used, n + 1)
                    if j:
                        act.wait_ge(y_done, j)
                    else:
                        act.wait_ge(ix_done, 8)
                    for q in range(4):
                        A.activation(gi[:, q, :], lru_bank(12 + j, q), ACT.Gelu_apprx_tanh,
                                     bias=col(1, B_IN + 4 * j + q)).then_inc(act_hi_done, 1)
                if s == 12:
                    stationary(0, 0, act_slot(0))
                split((n + 4) // 4, s % 4)

            down(0)
            up(0, C_UP0, 0)
            stationary(1, 0, act_slot(0))
            down(1)

            for j in range(8):
                if j == 0:
                    act_tiles(1, 3)
                    act.wait_ge(hT_copied, 8)
                    act.wait_ge(act_lo_done, LO0[1] + 16)
                act.wait_ge(chunk_used, C_DKV + j + 1)
                for k in (2 * j, 2 * j + 1):
                    A.activation(act_hi[:, k, :], feat[:, k, :], ACT.Copy,
                                 scale=col(0, G_MIX1 + k)).then_inc(act_hi_done, 1)
                if j == 7:
                    act.wait_ge(rstd_done, 3)
                    act.wait_ge(act_lo_done, LO0["mix"] + 16)
                    for t in range(NT):
                        for hf in range(2):
                            A.activation(ckr[:, t, hf * HALF:(hf + 1) * HALF], ps[2 * hf + t][:, 0:HALF], ACT.Copy,
                                         scale=stat(RS + 4 + t)).then_inc(ckr_done, 1)
                    act.wait_ge(ckr_done, 4)
                    act.wait_ge(h_sq, 2 * NB)
                    for t in range(NT):
                        A.activation(junk[:, t, :], ckr[:, t, 0:KV_LORA], ACT.Square, accum_out=stat(SS_C + t))
                        i = A.activation(gtmp[:, t, 0:ROPE], ckr[:, t, KV_LORA:DKV], ACT.Square,
                                         accum_out=stat(SS_KR + t))
                    i.then_inc(c_sq, 1)
                split((C_DKV + j + 4) // 4, j % 4)

            def latent_hi(i, g0):
                act.wait_ge(cT_mm, i + 1)
                for q in range(LT):
                    A.activation(act_hi[:, 4 * i + q, :], latent_psum(i, q), ACT.Copy,
                                 scale=col(0, g0 + q)).then_inc(c_hi, 1)

            for j in range(4):
                if j == 1:
                    latent_hi(0, G_CKV)
                if j == 3:
                    act.wait_ge(chunk_used, C_DQ + 4)
                    for t in range(NT):
                        A.activation(cq[:, t, :], ps[4 + t][:, :], ACT.Copy,
                                     scale=stat(RS + 4 + t)).then_inc(cq_done, 1)
                    act.wait_ge(cq_done, 2)
                    act.wait_ge(c_sq, 1)
                    for t in range(NT):
                        i = A.activation(junk[:, t, :], cq[:, t, :], ACT.Square, accum_out=stat(SS_Q + t))
                    i.then_inc(c_sq, 1)
                split((C_DQ + j + 4) // 4, j)

            def pair(m, u, live=True, mid=True, old=True, first=False):
                p = 2 * m + u
                if old:
                    act.wait_ge(s_max, p - 1)
                    for e in range(2):
                        for t in range(NT):
                            sl = prob(e, t)
                            i = A.activation(sl, sl, ACT.Exp, bias=stat(NMX + 2 * e + t),
                                             accum_out=stat(PSUMS + 2 * e + t))
                    i.then_inc(s_exp, 1)
                if live:
                    act.wait_ge(chunk_used, 2 * p + (C_PAIR + 1))
                    if not first:
                        act.wait_ge(q_ss, p)
                    for t in range(NT):
                        i = A.activation(sq[:, t, :, 0:NOPE], kv_psum(t)[:, :, 0:NOPE], ACT.Square)
                    i.then_inc(k_sq, 1)
                    if first:
                        latent_hi(1, G_CQ)
                    split(m + (C_PAIR // 4 + 1), 2 * u)
                if mid:
                    act.wait_ge(t_mm, p)
                    A.activation(knT[:, :, :].rearrange("p e s -> p (e s)"), ps[4][:, :], ACT.Copy, scale=col(0, G_KN))
                    A.activation(qnT[:, :, :].rearrange("p e s -> p (e s)"), ps[5][:, :], ACT.Copy,
                                 scale=col(0, G_QN)).then_inc(t_act, 1)
                if old:
                    act.wait_ge(pt_mm, p - 1)
                    A.activation(pT[:, 0, :], ps[7][:, 0:3 * P], ACT.Copy).then_inc(pt_act, 1)
                if live:
                    act.wait_ge(chunk_used, 2 * p + (C_PAIR + 2))
                    act.wait_ge(k_ss, p + 1)
                    for t in range(NT):
                        i = A.activation(sq[:, t, :, :], q_psum(t), ACT.Square)
                    i.then_inc(q_sq, 1)
                    split(m + (C_PAIR // 4 + 1), 2 * u + 1)
                if old:
                    act.wait_ge(o_mm, p - 1)
                    A.activation(feat[:, bass.ds(2 * p - 4, 2), :], ps[7][:, :].rearrange("p (e s) -> p e s", e=2),
                                 ACT.Copy).then_inc(o_done, 1)
                if live:
                    act.wait_ge(k_norm, p + 1)
                    for t in range(NT):
                        i = A.activation(v_sb[:, u, t, :, :], kv_psum(t)[:, :, NOPE:NOPE + VD], ACT.Copy)
                    i.then_inc(v_done, 1)

            pair(0, 0, mid=False, old=False, first=True)
            pair(0, 1, old=False)
            with act.Fori(1, PAIRS // 2) as m:
                pair(m, 0)
                pair(m, 1)
            pair(PAIRS // 2, 0, live=False)
            stationary(2, 0, act_slot(0))
            pair(PAIRS // 2, 1, live=False, mid=False)

            down(2)
            up(1, C_UP1, 2)
            stationary(3, 0, act_slot(0))
            down(3)

        @block.vector
        def _(dve):
            V = nc.vector

            def split(m, s):
                if isinstance(m, int) and 4 * m + s >= CHUNKS:
                    return
                size = chunk_size(4 * m + s) if isinstance(m, int) else KC * W
                dve.wait_ge(w_hi_done, 4 * m + s + 1)
                V.tensor_tensor(flat_chunk(w_lo, s, size), flat_chunk(raw, s, size),
                                flat_chunk(w_hi, s, size).bitcast(F32), ALU.subtract).then_inc(w_lo_done, 1)

            def lo_tile(k, src, g):
                return V.scalar_tensor_tensor(out=act_lo[:, k, :], in0=src, scalar=g,
                                              in1=act_hi[:, k, :].bitcast(F32), op0=ALU.mult, op1=ALU.subtract)

            def act_tiles(kind, b):
                for q in range(4):
                    k = 4 * b + q
                    if q % 2 == 0:
                        dve.wait_ge(act_hi_done, HI0[kind] + k + 2)
                        if kind == 1:
                            dve.wait_ge(hT_copied, k // 2 + 1)
                    lo_tile(k, hT_psum(b, q), col(0, gain[kind] + k)).then_inc(act_lo_done, 1)

            def update(d, b):
                dve.wait_ge(chunk_used, DOWN_C[d] + 4 * (DOWN_G[d] - 1) + b + 1)
                if d == 0 and b == 0:
                    dve.wait_ge(bout_added, 1)
                for t in range(NT):
                    hb = h[:, t, b * W:(b + 1) * W]
                    i = V.tensor_tensor(hb, hb, ps[2 * b + t][:, :], ALU.add)
                i.then_inc(h_done, 1)

            def stationary(g, slot, n):
                dve.wait_ge(st_hi, n)
                V.tensor_tensor(act_lo[:, slot:slot + 4, :], feat[:, bass.ds(4 * g, 4), :],
                                act_hi[:, slot:slot + 4, :].bitcast(F32), ALU.subtract).then_inc(st_lo, 1)

            def gT_out(i, n):
                dve.wait_ge(gT_mm, n)
                V.tensor_copy(feat[:, bass.ds(4 * i + 2, 2), :],
                              ps[5][:, :].rearrange("p (a b) -> p a b", a=2)).then_inc(gT_dve, 1)

            def down(d):
                def group(g, slot_next, last=False):
                    for b in range(NB):
                        if b == 0 and isinstance(g, int) and g == 0 and d in (1, 3):
                            gT_out(FB - 1, FB * (d // 2) + FB)
                        if b == 0 and not last:
                            stationary(g + 1, slot_next, g + (DOWN_G0[d] + 2))
                        if last:
                            update(d, b)
                            if d < 3 and b >= 1:
                                act_tiles(d, b - 1)
                        split(g + (DOWN_C[d] // 4 + 1), b)

                if DOWN_G[d] > 4:
                    group(0, act_slot(1))
                    group(1, act_slot(2))
                    with dve.Fori(0, (DOWN_G[d] - 3) // 2) as i:
                        for u in range(2):
                            group(2 * i + (2 + u), act_slot(3 + u))
                else:
                    for g in range(DOWN_G[d] - 1):
                        group(g, act_slot(g + 1))
                group(DOWN_G[d] - 1, None, last=True)
                if d < 3:
                    dve.wait_ge(h_sq, NB * (d + 1))
                    dve.wait_ge(rstd_done, d + 1)
                    V.tensor_reduce(stat(SS_T, 2), stat(SS_D, NT * NB).rearrange("p (t b) -> p t b", t=NT),
                                    AX.X, ALU.add).then_inc(ms_done, 1)

            def up(f, c0, d):
                def body(i, first):
                    for c in range(8):
                        if c == 0 and first:
                            act_tiles(d, 3)
                        if c == 0 and not first:
                            gT_out(i - 1, i + FB * f)
                        if c == 7:
                            dve.wait_ge(chunk_used, 8 * i + (c0 + 8))
                            dve.wait_ge(silu_done, i + (FB * f + 1))
                            for t in range(NT):
                                k = V.scalar_tensor_tensor(out=gtmp[:, t, :], in0=ps[2 + t][:, :],
                                                           scalar=stat(RS + 2 * (d + 1) + t), in1=gtmp[:, t, :],
                                                           op0=ALU.mult, op1=ALU.mult)
                            k.then_inc(g_done, 1)
                        split(2 * i + ((c0 + c + 4) // 4), c % 4)

                body(0, True)
                with dve.Fori(1, FB) as i:
                    body(i, False)

            n_prep = [0]

            def step(ins):
                n_prep[0] += 1
                ins.then_inc(prep, 1)
                dve.wait_ge(prep, n_prep[0])

            dve.wait_ge(vec_in, VEC_ALL)
            step(V.tensor_copy(posf[:, :], posi[:, :]))
            for t in range(NT):
                step(V.tensor_scalar(ang[:, 0, t, :], invf[:, :], posf[:, t:t + 1], None, ALU.mult))
            dve.wait_ge(x_in[1], 16)
            V.tensor_tensor_reduce(xn[:, 1, :], h[:, 1, :], h[:, 1, :], 1.0, 0.0, ALU.mult, ALU.add,
                                   stat(SS_X + 1)).then_inc(x_sq, 1)

            def reduce_angle(dst, tmp, shift, quarter):
                r, n = ang[:, dst, :, :], ang[:, tmp, :, :]
                step(V.tensor_scalar(r, ang[:, 0, :, :], float(1 / (2 * np.pi)), shift, ALU.mult, ALU.add))
                step(V.tensor_scalar(n, r, 12582912.0, None, ALU.add))
                step(V.tensor_scalar(n, n, -12582912.0, None, ALU.add))
                step(V.scalar_tensor_tensor(out=r, in0=n, scalar=-TWO_PI[0], in1=ang[:, 0, :, :],
                                            op0=ALU.mult, op1=ALU.add))
                for part in TWO_PI[1:]:
                    step(V.scalar_tensor_tensor(out=r, in0=n, scalar=-part, in1=r, op0=ALU.mult, op1=ALU.add))
                step(V.tensor_scalar(r, r, quarter, PI_DOWN, ALU.add, ALU.min))
                step(V.tensor_scalar(r, r, -PI_DOWN, None, ALU.max))

            for r, n_rows in enumerate((ROWS_A, ROWS_B, ROWS_C)):
                dve.wait_ge(cols_mm, r + 1)
                V.tensor_copy(cols[:, r, 0:n_rows], ps[r][:, 0:n_rows]).then_inc(cols_done, 1)
            dve.wait_ge(rstd_done, 1)
            for t in range(NT):
                V.tensor_scalar(xn[:, t, :], h[:, t, :], stat(RS + t), None, ALU.mult).then_inc(xn_done, 1)
            for s in range(2):
                split(0, s)
            for b in range(NB):
                act_tiles("x", b)
                if b == 1:
                    for s in (2, 3):
                        split(0, s)

            def rec_lo_block(n):
                dve.wait_ge(rec_hi, n + 1)
                V.tensor_tensor(rec_split[:, n % 4, 1, :, :], feat[:, 2 * n:2 * n + 2, :],
                                rec_split[:, n % 4, 0, :, :].bitcast(F32), ALU.subtract).then_inc(rec_lo, 1)

            def convolve(j):
                for w in (3, 2, 1, 0):
                    for q in range(4):
                        k = 4 * j + q
                        tap = col(1, CONV_W + KT * w + k)
                        src, dst = utmp[:, q, w:w + SEQ], feat[:, k, :]
                        if w == 3:
                            dve.wait_ge(act_hi_done, HI0["lru"] + k + 1)
                            i = V.tensor_scalar(dst, src, tap, col(1, CONV_B + k), ALU.mult, ALU.add)
                        else:
                            dve.wait_ge(conv_step, 12 * j + 4 * (2 - w) + q + 1)
                            i = V.scalar_tensor_tensor(out=dst, in0=src, scalar=tap, in1=dst,
                                                       op0=ALU.mult, op1=ALU.add)
                        if w:
                            i.then_inc(conv_step, 1)
                i.then_inc(conv_done, 1)

            for n in range(C_REC, C_GATE):
                if n == 0:
                    dve.wait_ge(cols_done, 3)
                    step(V.scalar_tensor_tensor(out=sp[:, 0, :], in0=cols[:, 2, LAM:LAM + KT], scalar=-1.0,
                                                in1=cols[:, 2, LAM:LAM + KT], op0=ALU.mult, op1=ALU.max))
                    V.tensor_scalar(neg_bg[:, :], cols[:, 2, B_GATE:B_GATE + 32], -1.0, None,
                                    ALU.mult).then_inc(neg_bg_done, 1)
                    V.tensor_scalar(sp[:, 2, :], cols[:, 2, LAM:LAM + KT], -1.0, 0.0, ALU.mult,
                                    ALU.max).then_inc(lam_done, 1)
                if n == 1:
                    dve.wait_ge(lam_exp, 1)
                    y, s1, s2, q1 = sp[:, 1, :], sp[:, 3, :], sp[:, 4, :], sp[:, 5, :]
                    step(V.tensor_scalar(s1, y, 2.0, None, ALU.add))
                    step(V.reciprocal(s1, s1))
                    step(V.tensor_tensor(s1, s1, y, ALU.mult))
                    step(V.tensor_tensor(s2, s1, s1, ALU.mult))
                    step(V.tensor_scalar(q1, s2, 1.0 / 15, None, ALU.mult))
                    for c in (13, 11, 9, 7, 5, 3):
                        step(V.scalar_tensor_tensor(out=q1, in0=q1, scalar=1.0 / c, in1=s2, op0=ALU.add, op1=ALU.mult))
                    step(V.scalar_tensor_tensor(out=q1, in0=q1, scalar=1.0, in1=s1, op0=ALU.add, op1=ALU.mult))
                    step(V.scalar_tensor_tensor(out=q1, in0=q1, scalar=2.0, in1=sp[:, 2, :], op0=ALU.mult, op1=ALU.add))
                    V.tensor_scalar(decay[:, 0, :], q1, -8.0, None, ALU.mult)
                    V.tensor_scalar(decay[:, 1, :], q1, 8.0, None, ALU.mult).then_inc(decay_done, 1)
                if n == 2:
                    reduce_angle(2, 1, 0.0, 0.0)
                    reduce_angle(4, 3, 0.25, float(np.pi / 2))
                    V.tensor_copy(posf[:, :], posi[:, :]).then_inc(angles_done, 1)
                if n % 4 == 3:
                    convolve(n // 4)
                if n in (7, 11):
                    rec_lo_block(n // 4 * 2 - 2)
                    rec_lo_block(n // 4 * 2 - 1)
                split((n + 4) // 4, n % 4)
            for c in range(4):
                for n in (2 * c, 2 * c + 1):
                    dve.wait_ge(act_hi_done, HI0["lru"] + 16 + 4 * (n + 1))
                    r2, i2 = feat[:, 16 + 2 * n:18 + 2 * n, :], gi[:, 2 * (n % 2):2 * (n % 2) + 2, :]
                    V.tensor_scalar(r2, r2, 1.0, None, ALU.add).then_inc(sig_step, 1)
                    V.tensor_scalar(i2, i2, 1.0, None, ALU.add).then_inc(sig_step, 1)
                    dve.wait_ge(sig_step, 2 * n + 1)
                    V.reciprocal(r2, r2)
                    dve.wait_ge(sig_step, 2 * n + 2)
                    V.reciprocal(i2, i2).then_inc(sig_done, 1)
                    if n + 4 < 8:
                        rec_lo_block(n + 4)
                split((C_GATE + c + 4) // 4, c)

            def gain_of_input(hb):
                t4, d4 = feat[:, 16 + 4 * hb:20 + 4 * hb, :], feat[:, 40:44, :]
                dve.wait_ge(tanh_done, 4 * hb + 4)
                if hb:
                    dve.wait_ge(z_done, hb)
                V.tensor_scalar(d4, t4, 1.0, None, ALU.add).then_inc(z_step, 1)
                dve.wait_ge(z_step, 3 * hb + 1)
                V.reciprocal(d4, d4).then_inc(z_step, 1)
                dve.wait_ge(z_step, 3 * hb + 2)
                V.scalar_tensor_tensor(out=t4, in0=t4, scalar=2.0, in1=d4, op0=ALU.mult, op1=ALU.mult).then_inc(z_step, 1)
                dve.wait_ge(z_step, 3 * hb + 3)
                V.tensor_scalar(t4, t4, 1e-34, None, ALU.max).then_inc(z_done, 1)

            def scans(bt):
                dve.wait_ge(sqrt_done, bt + 1)
                dve.wait_ge(ix_done, 4 * (bt + 1))
                s8 = feat[:, 16 + 8 * bt:24 + 8 * bt, :]
                V.tensor_tensor(s8, s8, feat[:, 8 * bt:8 * bt + 8, :], ALU.mult).then_inc(b_done, 1)
                dve.wait_ge(b_done, bt + 1)
                for k in range(8 * bt, 8 * bt + 8):
                    V.tensor_tensor_scan(feat[:, k, :], feat[:, 32 + k % 8, :], feat[:, 16 + k, :], 0.0,
                                         ALU.mult, ALU.add).then_inc(scan_done, 1)

            for s in range(16):
                n = C_GEL + s
                if s in (1, 2, 5, 6):
                    gain_of_input({1: 0, 2: 1, 5: 2, 6: 3}[s])
                if s in (3, 7):
                    scans(s // 4)
                if s % 4 == 3:
                    j = s // 4
                    dve.wait_ge(act_hi_done, HI0["lru"] + 48 + 4 * (j + 1))
                    dve.wait_ge(scan_done, 4 * (j + 1))
                    y4 = feat[:, 4 * j:4 * j + 4, :]
                    V.tensor_tensor(y4, y4, gi[:, :, :], ALU.mult).then_inc(y_done, 1)
                if s == 12:
                    stationary(0, act_slot(0), 1)
                split((n + 4) // 4, s % 4)

            down(0)
            up(0, C_UP0, 0)
            stationary(0, act_slot(0), DOWN_G0[1] + 1)
            down(1)

            for j in range(8):
                if j == 0:
                    act_tiles(1, 3)
                for k in (2 * j, 2 * j + 1):
                    dve.wait_ge(act_hi_done, HI0["mix"] + k + 1)
                    lo_tile(k, feat[:, k, :], col(0, G_MIX1 + k)).then_inc(act_lo_done, 1)
                split((C_DKV + j + 4) // 4, j % 4)
            dve.wait_ge(ckr_done, 4)
            dve.wait_ge(rope_done, 1)
            kraw = ckr[:, :, KV_LORA:DKV]
            V.tensor_tensor(rot_k[:, :, 0:32], kraw[:, :, 32:64], rope_s[:, 0, :, 0:32], ALU.mult)
            V.tensor_tensor(rot_k[:, :, 32:64], kraw[:, :, 0:32], rope_s[:, 0, :, 32:64], ALU.mult)
            V.tensor_tensor(kr_all[:, :, :], kraw, rope_c[:, 0, :, :], ALU.mult).then_inc(kr_step, 1)
            dve.wait_ge(kr_step, 1)
            V.tensor_tensor(kr_all[:, :, :], kr_all[:, :, :], rot_k[:, :, :], ALU.add).then_inc(kr_step, 1)
            dve.wait_ge(kr_step, 2)

            def latent_norm(i, buf, rs):
                dve.wait_ge(c_rstd, i + 1)
                for t in range(NT):
                    k = V.tensor_scalar(buf[:, t, 0:KV_LORA], buf[:, t, 0:KV_LORA], stat(rs + t), None, ALU.mult)
                k.then_inc(c_norm, 1)

            def latent_lo(i, g0):
                for q in range(LT):
                    if q % 2 == 0:
                        dve.wait_ge(c_hi, LT * i + q + 2)
                    lo_tile(4 * i + q, latent_psum(i, q), col(0, g0 + q)).then_inc(c_lo, 1)

            latent_norm(0, ckr, RS_C)
            for j in range(4):
                if j == 1:
                    latent_lo(0, G_CKV)
                if j == 3:
                    latent_norm(1, cq, RS_Q)
                split((C_DQ + j + 4) // 4, j)

            def pair(m, u, live=True, mid=True, old=True, first=False):
                p = 2 * m + u
                if old:
                    dve.wait_ge(s_mm, p - 1)
                    V.memset(stat(WAIT_SLOT), 0.0)
                    for e in range(2):
                        for t in range(NT):
                            i = V.tensor_tensor_reduce(prob(e, t), score_psum(e, t), mask_of(t), SCALE, -3e38,
                                                       ALU.add, ALU.max, stat(MX + 2 * e + t))
                    i.then_inc(s_step, 1)
                    dve.wait_ge(s_step, 2 * p - 3)
                    V.tensor_scalar(stat(NMX, 4), stat(MX, 4), -1.0, None, ALU.mult).then_inc(s_max, 1)
                    dve.wait_ge(s_exp, p - 1)
                    V.reciprocal(stat(RPS, 4), stat(PSUMS, 4)).then_inc(s_step, 1)
                    dve.wait_ge(s_step, 2 * p - 2)
                    for e in range(2):
                        for t in range(NT):
                            i = V.tensor_scalar(prob(e, t), prob(e, t), stat(RPS + 2 * e + t), None, ALU.mult)
                    i.then_inc(p_done, 1)
                if live:
                    if first:
                        latent_lo(1, G_CQ)
                    split(m + (C_PAIR // 4 + 1), 2 * u)
                    dve.wait_ge(k_sq, p + 1)
                    V.tensor_reduce(stat(SS_K, 4), sq[:, :, :, 0:NOPE], AX.X, ALU.add).then_inc(k_ss, 1)
                if mid:
                    dve.wait_ge(t_mm, p)
                    V.tensor_copy(krT[:, :], ps[6][:, 0:SEQ])
                    for e in range(2):
                        rows_e = slice(e * ROPE, (e + 1) * ROPE)
                        i = V.tensor_copy(qrT[rows_e, e, :], ps[6][rows_e, SEQ:2 * SEQ])
                    i.then_inc(t_dve, 1)
                if old:
                    dve.wait_ge(pt_mm, p - 1)
                    V.tensor_copy(pT[:, 1, :], ps[2][:, 0:3 * P]).then_inc(pt_dve, 1)
                if live:
                    dve.wait_ge(k_rs, p + 1)
                    for t in range(NT):
                        rs = stat(RS_K + 2 * t, 2)[:, :, None]
                        V.tensor_tensor(kn[:, t, :, :], kv_psum(t)[:, :, 0:NOPE], rs.broadcast_to([P, 2, NOPE]),
                                        ALU.mult)
                        i = V.tensor_tensor(kr[:, t, :, :], kr_all[:, t, None, :].broadcast_to([P, 2, ROPE]),
                                            rs.broadcast_to([P, 2, ROPE]), ALU.mult)
                    i.then_inc(k_norm, 1)
                    split(m + (C_PAIR // 4 + 1), 2 * u + 1)
                    dve.wait_ge(q_sq, p + 1)
                    V.tensor_reduce(stat(SS_QH, 4), sq[:, :, :, :], AX.X, ALU.add).then_inc(q_ss, 1)
                    dve.wait_ge(q_rs, p + 1)
                    for t in range(NT):
                        rs = stat(RS_QH + 2 * t, 2)[:, :, None]
                        i = V.tensor_tensor(qn[:, t, :, :], q_psum(t), rs.broadcast_to([P, 2, QK]), ALU.mult)
                    i.then_inc(q_step, 1)
                    dve.wait_ge(q_step, 2 * p + 1)
                    for t in range(NT):
                        sn = rope_s[:, 1, t, None, :].broadcast_to([P, 2, ROPE])
                        cs = rope_c[:, 1, t, None, :].broadcast_to([P, 2, ROPE])
                        V.tensor_tensor(rot[:, t, :, 0:32], qn[:, t, :, NOPE + 32:QK], sn[:, :, 0:32], ALU.mult)
                        V.tensor_tensor(rot[:, t, :, 32:64], qn[:, t, :, NOPE:NOPE + 32], sn[:, :, 32:64], ALU.mult)
                        i = V.tensor_tensor(qr[:, t, :, :], qn[:, t, :, NOPE:QK], cs, ALU.mult)
                    i.then_inc(q_step, 1)
                    dve.wait_ge(q_step, 2 * p + 2)
                    V.tensor_tensor(qr[:, :, :, :].rearrange("p t e d -> p (t e d)"),
                                    qr[:, :, :, :].rearrange("p t e d -> p (t e d)"),
                                    rot[:, :, :, :].rearrange("p t e d -> p (t e d)"), ALU.add).then_inc(q_norm, 1)

            pair(0, 0, mid=False, old=False, first=True)
            pair(0, 1, old=False)
            with dve.Fori(1, PAIRS // 2) as m:
                pair(m, 0)
                pair(m, 1)
            pair(PAIRS // 2, 0, live=False)
            stationary(0, act_slot(0), DOWN_G0[2] + 1)
            pair(PAIRS // 2, 1, live=False, mid=False)

            down(2)
            up(1, C_UP1, 2)
            stationary(0, act_slot(0), DOWN_G0[3] + 1)
            down(3)

        @block.gpsimd
        def _(pool):
            G = nc.gpsimd
            n_pool = [0]

            def step(ins):
                n_pool[0] += 1
                ins.then_inc(pool_step, 1)
                pool.wait_ge(pool_step, n_pool[0])

            G.memset(minus_half[:, :], -0.5)
            G.memset(stat(QK_EPS4, 4), QK * EPS)
            G.memset(stat(INV_QK4, 4), 1.0 / QK)
            G.memset(utmp[:, :, 0:3], 0.0)
            G.memset(ident[:, :], 0.0)
            step(G.memset(mask[:, :], 0.0))
            G.affine_select(out=ident[:, :], in_=ident[:, :], compare_op=ALU.not_equal, fill=1.0, base=0,
                            pattern=[[-1, P]], channel_multiplier=1)
            for c in (0, 2):
                tri = mask[:, c * P:(c + 1) * P]
                i = G.affine_select(out=tri, in_=tri, compare_op=ALU.is_ge, fill=NEG, base=0,
                                    pattern=[[-1, P]], channel_multiplier=1)
            i.then_inc(consts, 1)

            def rstd(ss, rs, n, width, signal):
                step(G.tensor_scalar(stat(rs, n), stat(ss, n), 1.0 / width, EPS, ALU.mult, ALU.add))
                G.tensor_tensor(stat(rs, n), stat(rs, n), minus_half[:, 0:n], ALU.pow).then_inc(signal, 1)

            pool.wait_ge(x_sq, 2)
            rstd(SS_X, RS, 2, D, rstd_done)
            pool.wait_ge(bout_in, 16)
            pool.wait_ge(xn_done, 2)
            for t in range(NT):
                i = G.tensor_tensor(h[:, t, :], h[:, t, :], bout[:, :], ALU.add)
            i.then_inc(bout_added, 1)
            pool.wait_ge(sin_done, 1)
            for kind in range(2):
                for t in range(NT):
                    for half in range(2):
                        cut = slice(32 * half, 32 * half + 32)
                        other = slice(32 - 32 * half, 64 - 32 * half)
                        G.tensor_tensor(rope_c[:, kind, t, cut], ang[:, 7, t, :], rope_g[:, kind, cut], ALU.mult)
                        i = G.tensor_tensor(rope_s[:, kind, t, cut], ang[:, 6 - half, t, :], rope_g[:, kind, other],
                                            ALU.mult)
            i.then_inc(rope_done, 1)
            for n in range(8):
                pool.wait_ge(sig_done, n + 1)
                G.tensor_tensor(feat[:, 2 * n:2 * n + 2, :], feat[:, 2 * n:2 * n + 2, :],
                                gi[:, 2 * (n % 2):2 * (n % 2) + 2, :], ALU.mult).then_inc(ix_done, 1)
            for d in (0, 1):
                pool.wait_ge(ms_done, d + 1)
                rstd(SS_T, RS + 2 * (d + 1), 2, D, rstd_done)
            pool.wait_ge(st_lo, DOWN_G0[2])
            pool.wait_ge(rstd_done, 3)
            step(G.memset(qrT[ROPE:P, 0, :], 0.0))
            step(G.memset(qrT[0:ROPE, 1, :], 0.0))
            G.memset(stat(POOL_SLOT), 0.0).then_inc(qz_done, 1)
            pool.wait_ge(c_sq, 1)
            rstd(SS_C, RS_C, 2, KV_LORA, c_rstd)
            for t in range(NT):
                for e in range(2):
                    step(G.tensor_scalar(stat(SS_KR4 + 2 * t + e), stat(SS_KR + t), 1.0, QK * EPS, ALU.mult, ALU.add))
            pool.wait_ge(c_sq, 2)
            rstd(SS_Q, RS_Q, 2, Q_LORA, c_rstd)
            with pool.Fori(0, PAIRS) as p:
                for n, (ss_ready, ss, more, rs, signal) in enumerate((
                        (k_ss, SS_K, SS_KR4, RS_K, k_rs), (q_ss, SS_QH, QK_EPS4, RS_QH, q_rs))):
                    pool.wait_ge(ss_ready, p + 1)
                    G.tensor_tensor(stat(rs, 4), stat(ss, 4), stat(more, 4), ALU.add).then_inc(pair_step, 1)
                    pool.wait_ge(pair_step, 4 * p + (2 * n + 1))
                    G.tensor_tensor(stat(rs, 4), stat(rs, 4), stat(INV_QK4, 4), ALU.mult).then_inc(pair_step, 1)
                    pool.wait_ge(pair_step, 4 * p + (2 * n + 2))
                    G.tensor_tensor(stat(rs, 4), stat(rs, 4), minus_half[:, 0:4], ALU.pow).then_inc(signal, 1)
            pool.wait_ge(ms_done, 3)
            rstd(SS_T, RS + 6, 2, D, rstd_done)

        @block.tensor
        def _(pe):
            T = nc.tensor

            def products(outs, k, t_of, s, kk, c0, width, first, last):
                for t in range(NT):
                    hi, lo = (buf[:, k, t * P:(t + 1) * P] for buf in (act_hi, act_lo))
                    passes = ((hi, w_hi), (hi, w_lo), (lo, w_hi))
                    for n, (x_part, w_part) in enumerate(passes):
                        wp = t_of(w_part, s, kk)[:, c0:c0 + width]
                        i = T.matmul(outs[t], x_part, wp, start=first and n == 0, stop=last and n == 2)
                return i

            def chunk_rows(buf, s, kk):
                return buf[:, s, kk, :]

            def chunk(m, s, outs, k0, first, last, width=W, rows_of=chunk_rows):
                pe.wait_ge(w_lo_done, 4 * m + s + 1)
                for kk in range(KC):
                    i = products(outs, k0 + kk, rows_of, s, kk, 0, width, first and kk == 0, last and kk == KC - 1)
                i.then_inc(chunk_used, 1)

            def transpose_h(d, b):
                pe.wait_ge(h_done, d * NB + b + 1)
                for q in range(4):
                    for t in range(NT):
                        k = 4 * b + q
                        i = T.transpose(hT_psum(b, q)[:, t * P:(t + 1) * P], h[:, t, k * P:(k + 1) * P], ident[:, :])
                i.then_inc(hT_mm, 1)

            def down(d):
                def group(g, slot, first=False, last=False):
                    for b in range(NB):
                        if b == 0:
                            pe.wait_ge(st_lo, g + (DOWN_G0[d] + 1))
                        if first:
                            if d == 0:
                                pe.wait_ge(act_hi_done, HI0[0] - 4 * (b < 2))
                            elif d in (1, 3) and b == 0:
                                pe.wait_ge(g_done, FB * (d // 2 + 1))
                            elif d in (1, 3) and b == 2:
                                pe.wait_ge(gT_act, FB * (d // 2 + 1))
                                pe.wait_ge(gT_dve, FB * (d // 2 + 1))
                            elif d == 2 and b == 0:
                                pe.wait_ge(v_done, PAIRS)
                                pe.wait_ge(p_done, PAIRS)
                                pe.wait_ge(pt_dve, PAIRS)
                            elif d == 2 and b == 3:
                                pe.wait_ge(o_done, PAIRS)
                        chunk(g + DOWN_C[d] // 4, b, (ps[2 * b][:, :], ps[2 * b + 1][:, :]), slot, first, last)
                        if first and b == 0 and d in (1, 3):
                            transpose_g(FB * (d // 2) + FB)
                        if last and d < 3 and b >= 1:
                            transpose_h(d, b - 1)

                if DOWN_G[d] > 4:
                    group(0, act_slot(0), first=True)
                    group(1, act_slot(1))
                    with pe.Fori(0, (DOWN_G[d] - 3) // 2) as i:
                        for u in range(2):
                            group(2 * i + (2 + u), act_slot(2 + u))
                else:
                    for g in range(DOWN_G[d] - 1):
                        group(g, act_slot(g), first=g == 0)
                group(DOWN_G[d] - 1, act_slot(DOWN_G[d] - 1), last=True)

            def transpose_g(n):
                pe.wait_ge(g_done, n)
                for q in range(4):
                    for t in range(NT):
                        i = T.transpose(ps[4 + q // 2][:, (q % 2) * SEQ + t * P:(q % 2) * SEQ + (t + 1) * P],
                                        gtmp[:, t, q * P:(q + 1) * P], ident[:, :])
                i.then_inc(gT_mm, 1)

            def up(f, c0, d):
                def body(i, first):
                    for c in range(8):
                        if first and c < 4:
                            pe.wait_ge(act_lo_done, LO0[d] + 4 * (c + 1))
                        if c == 0 and not first:
                            pe.wait_ge(silu_done, i + FB * f)
                        if c == 4 and not first:
                            pe.wait_ge(g_done, i + FB * f)
                        bank = 2 * (c // 4)
                        chunk(2 * i + ((c0 + c) // 4), c % 4, (ps[bank][:, :], ps[bank + 1][:, :]), 4 * (c % 4),
                              c % 4 == 0, c % 4 == 3)
                        if c == 0 and first:
                            transpose_h(d, 3)
                        if c == 0 and not first:
                            transpose_g(i + FB * f)

                body(0, True)
                with pe.Fori(1, FB) as i:
                    body(i, False)

            pe.wait_ge(consts, 1)
            pe.wait_ge(vec_in, VEC_ALL)
            for r, n_rows in enumerate((ROWS_A, ROWS_B, ROWS_C)):
                T.transpose(ps[r][:, 0:n_rows], rows[0:n_rows, r, :], ident[0:n_rows, 0:n_rows]).then_inc(cols_mm, 1)
            pe.wait_ge(cols_done, 3)
            pe.wait_ge(xn_done, 2)
            for k in range(KT):
                for t in range(NT):
                    i = T.transpose(hT_psum(k // 4, k % 4)[:, t * P:(t + 1) * P], xn[:, t, k * P:(k + 1) * P], ident[:, :])
                if k % 2:
                    i.then_inc(xT_mm, 1)

            def lru_tiles(idx, s, kks, move, first, last):
                for kk in kks:
                    x_hi, x_lo = move(kk)
                    for q in range(4):
                        wh, wl = (buf[:, s, kk, q * P:(q + 1) * P] for buf in (w_hi, w_lo))
                        for n, (w_part, x_part) in enumerate(((wh, x_hi), (wh, x_lo), (wl, x_hi))):
                            i = T.matmul(lru_bank(idx, q), w_part, x_part, start=first and kk == kks[0] and n == 0,
                                         stop=last and kk == kks[-1] and n == 2)
                return i

            def in_block(idx, m, first):
                for s in range(4):
                    if first:
                        pe.wait_ge(act_lo_done, max(8, 4 * (s + 1)))
                    pe.wait_ge(w_lo_done, 4 * m + s + 1)
                    lru_tiles(idx, s, range(4), lambda kk: (act_hi[:, 4 * s + kk, :], act_lo[:, 4 * s + kk, :]),
                              s == 0, s == 3).then_inc(chunk_used, 1)

            for j in range(NB):
                if j >= 2:
                    pe.wait_ge(act_hi_done, HI0["lru"] + 4 * (j - 1))
                in_block(j, j, j == 0)
            for n in range(8):
                pe.wait_ge(act_hi_done, HI0["lru"] + 4 * (n + 3))
                pe.wait_ge(rec_lo, n + 1)
                pe.wait_ge(w_lo_done, C_GATE + n // 2 + 1)
                kks = (2 * (n % 2), 2 * (n % 2) + 1)
                i = lru_tiles(4 + n, n // 2, kks, lambda kk: (rec_split[:, n % 4, 0, kk % 2, :],
                                                              rec_split[:, n % 4, 1, kk % 2, :]), True, True)
                i.then_inc(chunk_used if n % 2 else gate_half, 1)
            with pe.Fori(0, NB // 2) as j2:
                for u in range(2):
                    pe.wait_ge(act_hi_done, 8 * j2 + (HI0["lru"] + 4 * (11 + u)))
                    in_block(u, 2 * j2 + (C_GEL // 4 + u), False)

            down(0)
            up(0, C_UP0, 0)
            down(1)

            for j in range(8):
                pe.wait_ge(act_lo_done, LO0[1] + max(8, 4 * (j // 2 + 1)))
                pe.wait_ge(w_lo_done, C_DKV + j + 1)
                for kk in range(2):
                    for hf in range(2):
                        def dkv_rows(buf, s, r):
                            return flat_chunk(buf, s, 2 * DKV)[:, r * DKV:(r + 1) * DKV]
                        i = products((ps[2 * hf][:, 0:HALF], ps[2 * hf + 1][:, 0:HALF]), 2 * j + kk, dkv_rows, j % 4,
                                     kk, hf * HALF, HALF, j + kk == 0, j == 7 and kk == 1)
                i.then_inc(chunk_used, 1)
                if j == 0:
                    transpose_h(1, 3)

            def transpose_latent(i, buf):
                pe.wait_ge(c_norm, i + 1)
                for q in range(LT):
                    for t in range(NT):
                        k = T.transpose(latent_psum(i, q)[:, t * P:(t + 1) * P], buf[:, t, q * P:(q + 1) * P], ident[:, :])
                k.then_inc(cT_mm, 1)

            for j in range(4):
                pe.wait_ge(act_lo_done, LO0["mix"] + 4 * (j + 1))
                chunk(C_DQ // 4, j, (ps[4][:, :], ps[5][:, :]), 4 * j, j == 0, j == 3)
                if j == 1:
                    transpose_latent(0, ckr)

            def q_rows(buf, s, kk):
                return flat_chunk(buf, s, KC * 2 * QK)[:, kk * 2 * QK:(kk + 1) * 2 * QK]

            def pair(m, u, live=True, mid=True, old=True, first=False):
                p = 2 * m + u
                if live:
                    if first:
                        pe.wait_ge(ckr_done, 4)
                        pe.wait_ge(c_lo, LT)
                    else:
                        pe.wait_ge(v_done, p)
                        pe.wait_ge(k_norm, p)
                    chunk(m + C_PAIR // 4, 2 * u, (ps[0][:, :], ps[1][:, :]), 0, True, True)
                    if first:
                        transpose_latent(1, cq)
                if mid:
                    pe.wait_ge(q_norm, p)
                    if old:
                        pe.wait_ge(s_max, p - 1)
                    if first or (isinstance(m, int) and p == 1):
                        pe.wait_ge(c_lo, 2 * LT)
                    for e in range(2):
                        for t in range(NT):
                            sl = slice(e * SEQ + t * P, e * SEQ + (t + 1) * P)
                            T.transpose(ps[4][:, sl], kn[:, t, e, :], ident[:, :])
                            T.transpose(ps[5][:, sl], qn[:, t, e, 0:NOPE], ident[:, :])
                    for t in range(NT):
                        T.transpose(ps[6][:, t * P:(t + 1) * P], kr[:, t, :, :].rearrange("p e d -> p (e d)"),
                                    ident[:, :])
                        i = T.transpose(ps[6][:, SEQ + t * P:SEQ + (t + 1) * P],
                                        qr[:, t, :, :].rearrange("p e d -> p (e d)"), ident[:, :])
                    i.then_inc(t_mm, 1)
                if old:
                    pe.wait_ge(p_done, p - 1)
                    for e in range(2):
                        for c in range(3):
                            i = T.transpose(ps[7 if e == 0 else 2][:, c * P:(c + 1) * P],
                                            probs[:, e, c * P:(c + 1) * P], ident[:, :])
                    i.then_inc(pt_mm, 1)
                if live:
                    if first:
                        pe.wait_ge(c_lo, 2 * LT)
                    if old:
                        pe.wait_ge(pt_dve, p - 1)
                    chunk(m + C_PAIR // 4, 2 * u + 1, (ps[2][:, 0:2 * QK], ps[3][:, 0:2 * QK]), LT, True, True,
                          2 * QK, q_rows)
                if old:
                    pe.wait_ge(pt_act, p - 1)
                    pe.wait_ge(pt_dve, p - 1)
                    for e in range(2):
                        T.matmul(ps[7][:, e * SEQ:(e + 1) * SEQ], v_sb[:, u, 0, e, :], pT[:, e, 0:SEQ],
                                 start=True, stop=False)
                        i = T.matmul(ps[7][:, e * SEQ + P:(e + 1) * SEQ], v_sb[:, u, 1, e, :], pT[:, e, SEQ:3 * P],
                                     start=False, stop=True)
                    i.then_inc(o_mm, 1)
                if mid:
                    pe.wait_ge(t_act, p)
                    pe.wait_ge(t_dve, p)
                    if isinstance(m, int) and p == 1:
                        pe.wait_ge(qz_done, 1)
                    for e in range(2):
                        for t in range(NT):
                            queries, keys = slice(t * P, (t + 1) * P), slice(0, (t + 1) * P)
                            T.matmul(score_psum(e, t), qnT[:, e, queries], knT[:, e, keys], start=True, stop=False)
                            i = T.matmul(score_psum(e, t), qrT[:, e, queries], krT[:, keys], start=False, stop=True)
                    i.then_inc(s_mm, 1)

            pair(0, 0, mid=False, old=False, first=True)
            pair(0, 1, old=False)
            with pe.Fori(1, PAIRS // 2) as m:
                pair(m, 0)
                pair(m, 1)
            pair(PAIRS // 2, 0, live=False)
            pair(PAIRS // 2, 1, live=False, mid=False)

            down(2)
            up(1, C_UP1, 2)
            down(3)


NAMES = ["x", "positions", "norm_mix", "norm_ffn", "lru_w_in", "lru_b_in", "lru_conv_w", "lru_conv_b", "lru_w_gate",
         "lru_b_gate", "lru_lambda", "lru_w_out", "lru_b_out", "kv_norm_in", "w_dkv", "kv_latent_norm", "w_ukv",
         "k_norm", "w_dq", "q_latent_norm", "w_uq", "q_norm", "w_o", "ffn_w_in", "ffn_w_out"]


def kernel(**inputs):
    import concourse.bacc as bacc
    from concourse.bass_utils import run_bass_kernel_spmd

    nc = bacc.Bacc("TRN2", target_bir_lowering=False, num_devices=1)
    arrays = {name: np.ascontiguousarray(inputs[name]) for name in NAMES}
    arrays["inv_freq"] = (10000.0 ** (-np.arange(0, ROPE, 2, dtype=np.float64) / ROPE)).astype(np.float32)[None, :]
    aps, feeds = {}, {}
    for name, arr in arrays.items():
        aps[name] = nc.dram_tensor(f"in_{name}", arr.shape, mybir.dt.from_np(arr.dtype), kind="ExternalInput").ap()
        feeds[f"in_{name}"] = arr
    out = nc.dram_tensor("out", (1, SEQ, D), F32, kind="ExternalOutput").ap()
    build_program(nc, aps, out)
    result = run_bass_kernel_spmd(nc, [feeds], core_ids=[0])
    return result.results[0]["out"]
```

```python
from contextlib import ExitStack

import numpy as np

import concourse.bass as bass
from concourse import mybir

F32 = mybir.dt.float32
F32R = mybir.dt.float32r
I32 = mybir.dt.int32
ALU = mybir.AluOpType
ACT = mybir.ActivationFunctionType
AX = mybir.AxisListType

P = 128
SEQ = 256
NT = SEQ // P
D = 2048
KT = D // P
FF = 5632
W = 512
KC = 4
FB = FF // W
NB = D // W
HEADS, NOPE, ROPE, QK, VD = 16, 128, 64, 192, 128
PAIRS = HEADS // 2
KV_LORA = Q_LORA = 512
DKV = KV_LORA + ROPE
HALF = DKV // 2
LT = KV_LORA // P
EPS = 1e-6
SCALE = 1.0 / float(np.sqrt(QK))
NEG = -1e30

C_REC = 0
C_GATE = C_REC + 16
C_GEL = C_GATE + 4
C_LOUT = C_GEL + 16
C_UP0 = C_LOUT + 16
C_DOWN0 = C_UP0 + 8 * FB
C_DKV = C_DOWN0 + 4 * FB
C_DQ = C_DKV + 8
C_PAIR = C_DQ + 4
C_WO = C_PAIR + 2 * PAIRS
C_UP1 = C_WO + 16
C_DOWN1 = C_UP1 + 8 * FB
CHUNKS = C_DOWN1 + 4 * FB

DOWN_C = (C_LOUT, C_DOWN0, C_WO, C_DOWN1)
DOWN_G = (4, FB, 4, FB)
DOWN_G0 = (0, 4, 4 + FB, 8 + FB)
HI0 = {"x": 0, "lru": 16, 0: 80, 1: 96, "mix": 112, 2: 128}
LO0 = {"x": 0, 0: 16, 1: 32, "mix": 48, 2: 64}

G_MIX0, G_FFN0, G_KV, G_MIX1, G_FFN1, G_CKV, G_CQ, G_KN, G_QN = 0, 16, 32, 48, 64, 80, 84, 88, 89
ROWS_A = 90
B_IN, CONV_W, CONV_B = 0, 32, 96
ROWS_B = 112
B_GATE, LAM = 0, 32
ROWS_C = 48


def act_slot(g):
    return 4 * g if g < 2 else 8 + 4 * (g % 2)


TWO_PI = (6.28125, float(np.floor((2 * np.pi - 6.28125) * 2 ** 20) / 2 ** 20))
TWO_PI += (float(2 * np.pi - sum(TWO_PI)),)
PI_DOWN = 3.1415925


def build_program(nc, a, out):
    x, positions = a["x"], a["positions"]
    ctx = ExitStack()
    with ctx:
        def sb(name, shape, dt=F32, stack=ctx):
            return stack.enter_context(nc.sbuf_tensor(name, shape, dt))

        def sem(name):
            return ctx.enter_context(nc.semaphore(name))

        h = sb("h", [P, NT, D])
        act_hi = sb("act_hi", [P, KT, SEQ], F32R)
        act_lo = sb("act_lo", [P, KT, SEQ], F32R)
        raw = sb("raw", [P, 4, KC, W])
        w_hi = sb("w_hi", [P, 4, KC, W], F32R)
        w_lo = sb("w_lo", [P, 4, KC, W], F32R)
        gtmp = sb("gtmp", [P, NT, W])
        utmp = sb("utmp", [P, 4, 260])
        ident = sb("ident", [P, P])
        mask = sb("mask", [P, 3 * P])
        cols = sb("cols", [P, 3, P])
        decay = sb("decay", [P, 2, KT])
        stats = sb("stats", [P, 80])
        minus_half = sb("minus_half", [P, 8])
        rope_c = sb("rope_c", [P, 2, NT, ROPE])
        rope_s = sb("rope_s", [P, 2, NT, ROPE])
        with nc.sbuf_tensor("feat", [P, 4 * FB, SEQ], F32) as feat:
            pass
        with ExitStack() as over:
            sb("feat_0_27", [P, 28, SEQ], F32, over)
            rec_split = sb("rec_split", [P, 4, 2, 2, SEQ], F32R, over)
        with ExitStack() as over:
            sb("feat_0_15", [P, 16, SEQ], F32, over)
            v_sb = sb("v_sb", [P, 2, NT, 2, VD], F32, over)
            kn = sb("kn", [P, NT, 2, NOPE], F32, over)
            kr = sb("kr", [P, NT, 2, ROPE], F32, over)
            qn = sb("qn", [P, NT, 2, QK], F32, over)
            qr = sb("qr", [P, NT, 2, ROPE], F32, over)
            rot = sb("rot", [P, NT, 2, ROPE], F32, over)
            kr_all = sb("kr_all", [P, NT, ROPE], F32, over)
            rot_k = sb("rot_k", [P, NT, ROPE], F32, over)
            knT = sb("knT", [P, 2, SEQ], F32, over)
            qnT = sb("qnT", [P, 2, SEQ], F32, over)
            krT = sb("krT", [P, SEQ], F32, over)
            qrT = sb("qrT", [P, 2, SEQ], F32, over)
            pT = sb("pT", [P, 2, 3 * P], F32, over)
        with ExitStack() as over:
            sb("feat_0_19", [P, 20, SEQ], F32, over)
            bout = sb("bout", [P, D], F32, over)
            rows = sb("rows", [P, 3, P], F32, over)
            posi = sb("posi", [P, NT], I32, over)
            invf = sb("invf", [P, 32], F32, over)
            rope_g = sb("rope_g", [P, 2, ROPE], F32, over)
            ang = sb("ang", [P, 8, NT, 32], F32, over)
            posf = sb("posf", [P, NT], F32, over)
            sp = sb("sp", [P, 6, KT], F32, over)
        feat = sb("feat_all", [P, 4 * FB, SEQ])
        flat = feat[:, :, :].rearrange("p a b -> p (a b)")
        xn = flat[:, 0:NT * D].rearrange("p (t d) -> p t d", t=NT)
        ckr = flat[:, 0:NT * DKV].rearrange("p (t d) -> p t d", t=NT)
        cq = flat[:, 5 * SEQ:5 * SEQ + NT * Q_LORA].rearrange("p (t d) -> p t d", t=NT)
        gi = gtmp[:, :, :].rearrange("p t w -> p (t w)").rearrange("p (a b) -> p a b", a=4)
        probs = utmp[:, :, :].rearrange("p a b -> p (a b)")[:, 0:2 * 3 * P].rearrange("p (e k) -> p e k", e=2)
        sq = gtmp[:, :, :].rearrange("p t w -> p (t w)")[:, 0:NT * 2 * QK].rearrange("p (t e d) -> p t e d", t=NT, e=2)
        junk = utmp[:, :, :].rearrange("p a b -> p (a b)")[:, 0:2 * W].rearrange("p (t w) -> p t w", t=NT)
        ps = [ctx.enter_context(nc.psum_tensor(f"bank{i}", [P, W], F32)) for i in range(8)]

        SS_X, SS_D, SS_T, RS = 0, 2, 10, 12
        SS_C, RS_C, SS_Q, RS_Q, SS_KR = 20, 22, 24, 26, 28
        SS_K, RS_K, SS_QH, RS_QH = 30, 34, 38, 42
        MX, NMX, PSUMS, RPS = 46, 50, 54, 58
        SS_KR4, QK_EPS4, INV_QK4, WAIT_SLOT, POOL_SLOT = 64, 68, 72, 76, 77

        x_in = [sem(f"x_in{t}") for t in range(NT)]
        vec_in = sem("vec_in")
        rope_in = sem("rope_in")
        bout_in = sem("bout_in")
        raw_in = [sem(f"raw_in{s}") for s in range(4)]
        w_hi_done = sem("w_hi_done")
        w_lo_done = sem("w_lo_done")
        chunk_used = sem("chunk_used")
        consts = sem("consts")
        cols_mm = sem("cols_mm")
        cols_done = sem("cols_done")
        prep = sem("prep")
        rope_done = sem("rope_done")
        x_sq = sem("x_sq")
        x_rstd = sem("x_rstd")
        xn_done = sem("xn_done")
        xT_mm = sem("xT_mm")
        bout_added = sem("bout_added")
        rstd_done = sem("rstd_done")
        ms_done = sem("ms_done")
        act_hi_done = sem("act_hi_done")
        act_lo_done = sem("act_lo_done")
        conv_step = sem("conv_step")
        rec_hi = sem("rec_hi")
        rec_lo = sem("rec_lo")
        gate_half = sem("gate_half")
        ix_done = sem("ix_done")
        a_done = sem("a_done")
        tanh_done = sem("tanh_done")
        z_done = sem("z_done")
        conv_done = sem("conv_done")
        angles_done = sem("angles_done")
        sin_done = sem("sin_done")
        lam_done = sem("lam_done")
        lam_exp = sem("lam_exp")
        decay_done = sem("decay_done")
        pair_step = sem("pair_step")
        q_norm = sem("q_norm")
        z_step = sem("z_step")
        sqrt_done = sem("sqrt_done")
        b_done = sem("b_done")
        scan_done = sem("scan_done")
        y_done = sem("y_done")
        st_hi = sem("st_hi")
        st_lo = sem("st_lo")
        h_done = sem("h_done")
        hT_mm = sem("hT_mm")
        hT_copied = sem("hT_copied")
        h_sq = sem("h_sq")
        silu_done = sem("silu_done")
        g_done = sem("g_done")
        gT_mm = sem("gT_mm")
        gT_act = sem("gT_act")
        gT_dve = sem("gT_dve")
        ckr_done = sem("ckr_done")
        c_sq = sem("c_sq")
        cq_sq = sem("cq_sq")
        c_rstd = sem("c_rstd")
        c_norm = sem("c_norm")
        cT_mm = sem("cT_mm")
        c_hi = sem("c_hi")
        c_lo = sem("c_lo")
        cq_done = sem("cq_done")
        kr_step = sem("kr_step")
        qz_done = sem("qz_done")
        k_sq = sem("k_sq")
        k_ss = sem("k_ss")
        k_rs = sem("k_rs")
        q_sq = sem("q_sq")
        q_ss = sem("q_ss")
        q_rs = sem("q_rs")
        pool_step = sem("pool_step")
        k_norm = sem("k_norm")
        q_step = sem("q_step")
        t_mm = sem("t_mm")
        t_act = sem("t_act")
        t_dve = sem("t_dve")
        s_mm = sem("s_mm")
        s_max = sem("s_max")
        s_step = sem("s_step")
        s_exp = sem("s_exp")
        p_done = sem("p_done")
        pt_mm = sem("pt_mm")
        pt_act = sem("pt_act")
        pt_dve = sem("pt_dve")
        v_done = sem("v_done")
        o_mm = sem("o_mm")
        o_done = sem("o_done")
        stored = sem("stored")

        block = ctx.enter_context(nc.Block())

        def vector_loads():
            yield rows[0:16, 0, :], a["norm_mix"][0].rearrange("(r c) -> r c", c=P)
            yield rows[16:32, 0, :], a["norm_ffn"][0].rearrange("(r c) -> r c", c=P)
            yield rows[32:48, 0, :], a["kv_norm_in"].rearrange("(r c) -> r c", c=P)
            yield rows[48:64, 0, :], a["norm_mix"][1].rearrange("(r c) -> r c", c=P)
            yield rows[64:80, 0, :], a["norm_ffn"][1].rearrange("(r c) -> r c", c=P)
            yield rows[80:84, 0, :], a["kv_latent_norm"].rearrange("(r c) -> r c", c=P)
            yield rows[84:88, 0, :], a["q_latent_norm"][0].rearrange("(r c) -> r c", c=P)
            yield rows[88:89, 0, :], a["k_norm"][0:NOPE].rearrange("(r c) -> r c", c=P)
            yield rows[89:90, 0, :], a["q_norm"][0, 0:NOPE].rearrange("(r c) -> r c", c=P)
            yield rows[0:32, 1, :], a["lru_b_in"][0].rearrange("(r c) -> r c", c=P)
            yield rows[32:96, 1, :], a["lru_conv_w"][0].rearrange("w (r c) -> (w r) c", c=P)
            yield rows[96:112, 1, :], a["lru_conv_b"][0].rearrange("(r c) -> r c", c=P)
            yield rows[0:32, 2, :], a["lru_b_gate"][0].rearrange("n (r c) -> (n r) c", c=P)
            yield rows[32:48, 2, :], a["lru_lambda"][0].rearrange("(r c) -> r c", c=P)

        def rope_loads():
            yield posi[:, :], positions[0].rearrange("(t p) -> p t", p=P)
            yield invf[:, :], a["inv_freq"][0:1, :].broadcast_to([P, 32])
            yield rope_g[:, 0, :], a["k_norm"][NOPE:QK].rearrange("(o d) -> o d", o=1).broadcast_to([P, ROPE])
            yield rope_g[:, 1, :], a["q_norm"][0:1, NOPE:QK].broadcast_to([P, ROPE])

        vec_loads, rope_in_loads = list(vector_loads()), list(rope_loads())
        VEC_ALL, ROPE_ALL = 16 * len(vec_loads), 16 * len(rope_in_loads)

        @block.sync
        def _(sp_):
            for t in range(NT):
                sp_.dma_start(h[:, t, :], x[0, t * P:(t + 1) * P, :]).then_inc(x_in[t], 16)

            def load(m, s, src, dst=None):
                if not (isinstance(m, int) and m == 0):
                    sp_.wait_ge(w_lo_done, 4 * m + s - 3)
                sp_.dma_start(raw[:, s, :, :] if dst is None else dst, src).then_inc(raw_in[s], 16)

            def tile_rows(w, r, c, width=W):
                return w[r:r + KC * P, :].rearrange("(k p) n -> p k n", p=P)[:, :, bass.ds(c, width)]

            w_in = a["lru_w_in"][0]
            for dst, src in vec_loads[:6]:
                sp_.dma_start(dst, src, allow_slow_non_contiguous=True).then_inc(vec_in, 16)
            for s in range(4):
                if s == 1:
                    sp_.wait_ge(vec_in, VEC_ALL)
                load(0, s, tile_rows(w_in, s * KC * P, D))
            with sp_.Fori(1, NB) as j:
                for s in range(4):
                    load(j + C_REC // 4, s, tile_rows(w_in, s * KC * P, j * W + D))
            gate_rows = a["lru_w_gate"][0].rearrange("n d e -> (n d) e")
            for s in range(4):
                load(C_GATE // 4, s, tile_rows(gate_rows, s * KC * P, 0))
            with sp_.Fori(0, NB) as j:
                for s in range(4):
                    load(j + C_GEL // 4, s, tile_rows(w_in, s * KC * P, j * W))

            def down(w, c0, groups):
                by_group = w.rearrange("(g k p) n -> p g k n", k=KC, p=P)
                with sp_.Fori(0, groups) as g:
                    for b in range(NB):
                        src = by_group[:, bass.ds(g, 1), :, b * W:(b + 1) * W]
                        load(g + c0 // 4, b, src.rearrange("p g k n -> p (g k) n"))

            def up(w, c0):
                with sp_.Fori(0, FB) as i:
                    for c in range(8):
                        col = i * W + (c // 4) * FF
                        load(2 * i + (c0 // 4 + c // 4), c % 4, tile_rows(w, (c % 4) * KC * P, col))

            down(a["lru_w_out"][0], C_LOUT, 4)
            up(a["ffn_w_in"][0], C_UP0)
            down(a["ffn_w_out"][0], C_DOWN0, FB)
            for j in range(8):
                src = a["w_dkv"][2 * j * P:(2 * j + 2) * P, :].rearrange("(k p) n -> p k n", p=P)
                dst = raw[:, j % 4, :, :].rearrange("p k n -> p (k n)")[:, 0:2 * DKV]
                load((C_DKV + j) // 4, j % 4, src, dst.rearrange("p (k n) -> p k n", k=2))
            for s in range(4):
                load(C_DQ // 4, s, tile_rows(a["w_dq"][0], s * KC * P, 0))
            w_ukv = a["w_ukv"].rearrange("c h d -> c (h d)")
            w_uq = a["w_uq"][0].rearrange("c h d -> c (h d)")
            with sp_.Fori(0, PAIRS // 2) as i:
                for u in range(2):
                    load(i + C_PAIR // 4, 2 * u, tile_rows(w_ukv, 0, i * (2 * W) + u * W))
                    dst = raw[:, 2 * u + 1, :, :].rearrange("p k n -> p (k n)")[:, 0:KC * 2 * QK]
                    load(i + C_PAIR // 4, 2 * u + 1, tile_rows(w_uq, 0, i * (4 * QK) + u * 2 * QK, 2 * QK),
                         dst.rearrange("p (k n) -> p k n", k=KC))
            down(a["w_o"][0], C_WO, 4)
            up(a["ffn_w_in"][1], C_UP1)
            down(a["ffn_w_out"][1], C_DOWN1, FB)
            out_v = out[0].rearrange("(t p) d -> p t d", p=P)
            for b in range(NB):
                sp_.wait_ge(h_done, 3 * NB + b + 1)
                sp_.dma_start(out_v[:, :, b * W:(b + 1) * W], h[:, :, b * W:(b + 1) * W]).then_inc(stored, 16)
            sp_.wait_ge(stored, 16 * NB)

        def col(row_tile, c):
            return cols[:, row_tile, c:c + 1]

        def stat(c, n=1):
            return stats[:, c:c + n]

        gain = {"x": G_MIX0, 0: G_FFN0, 1: G_KV, "mix": G_MIX1, 2: G_FFN1}

        def hT_psum(b, q):
            return ps[2 * b + q // 2][:, (q % 2) * SEQ:(q % 2 + 1) * SEQ]

        def lru_bank(idx, q):
            return ps[4 * (idx % 2) + q][:, 0:SEQ]

        def latent_psum(i, q):
            return ps[6 - 2 * i + q // 2][:, (q % 2) * SEQ:(q % 2 + 1) * SEQ]

        def kv_psum(t):
            return ps[t][:, :].rearrange("p (e d) -> p e d", e=2)

        def q_psum(t):
            return ps[2 + t][:, 0:2 * QK].rearrange("p (e d) -> p e d", e=2)

        def seen(t):
            return slice(0, P) if t == 0 else slice(P, 3 * P)

        def score_psum(e, t):
            return ps[4 + e][:, seen(t)]

        def prob(e, t):
            return probs[:, e, seen(t)]

        def mask_of(t):
            return mask[:, 0:P] if t == 0 else mask[:, P:3 * P]

        def gate_block_done(eng, n):
            if n % 2:
                eng.wait_ge(chunk_used, C_GATE + n // 2 + 1)
            else:
                eng.wait_ge(gate_half, n // 2 + 1)

        def source_ready(eng, d, g):
            if d == 0:
                eng.wait_ge(y_done, g + 1)
            elif d == 2:
                eng.wait_ge(o_done, 2 * g + 2)
            else:
                f0 = FB * (d // 2)
                eng.wait_ge(gT_act, g + (f0 + 1))
                eng.wait_ge(gT_dve, g + (f0 + 1))

        def chunk_size(n):
            return 2 * DKV if C_DKV <= n < C_DQ else KC * W

        def flat_chunk(buf, s, size):
            return buf[:, s, :, :].rearrange("p k n -> p (k n)")[:, 0:size]

        @block.scalar
        def _(act):
            A = nc.scalar

            def split(m, s):
                if isinstance(m, int) and 4 * m + s >= CHUNKS:
                    return
                size = chunk_size(4 * m + s) if isinstance(m, int) else KC * W
                act.wait_ge(raw_in[s], 16 * m + 16)
                if not (isinstance(m, int) and m == 0):
                    act.wait_ge(chunk_used, 4 * m + s - 3)
                A.activation(flat_chunk(w_hi, s, size), flat_chunk(raw, s, size), ACT.Copy).then_inc(w_hi_done, 1)

            def act_tiles(kind, b):
                if kind != "x":
                    act.wait_ge(hT_mm, kind * NB + b + 1)
                for q in range(4):
                    k = 4 * b + q
                    if kind == "x" and q % 2 == 0:
                        act.wait_ge(xT_mm, k // 2 + 1)
                    A.activation(act_hi[:, k, :], hT_psum(b, q), ACT.Copy,
                                 scale=col(0, gain[kind] + k)).then_inc(act_hi_done, 1)
                    if kind == 1 and q % 2:
                        A.activation(feat[:, k - 1:k + 1, :].rearrange("p a b -> p (a b)"), ps[2 * b + q // 2][:, :],
                                     ACT.Copy).then_inc(hT_copied, 1)

            def squares(d, b):
                act.wait_ge(h_done, d * NB + b + 1)
                if d + b:
                    act.wait_ge(h_sq, d * NB + b)
                for t in range(NT):
                    i = A.activation(junk[:, t, :], h[:, t, b * W:(b + 1) * W], ACT.Square,
                                     accum_out=stat(SS_D + NB * t + b))
                i.then_inc(h_sq, 1)

            def stationary(d, g, slot):
                source_ready(act, d, g)
                if not isinstance(g, int) or g >= 4:
                    act.wait_ge(chunk_used, 4 * g + (DOWN_C[d] - 4))
                elif d == 2:
                    act.wait_ge(chunk_used, DOWN_C[d] - (g == 0))
                else:
                    act.wait_ge(chunk_used, DOWN_C[d] - 3 + g)
                A.activation(act_hi[:, slot:slot + 4, :], feat[:, bass.ds(4 * g, 4), :], ACT.Copy).then_inc(st_hi, 1)

            def gT_out(i, n):
                act.wait_ge(gT_mm, n)
                A.activation(feat[:, bass.ds(4 * i, 2), :], ps[4][:, :].rearrange("p (a b) -> p a b", a=2),
                             ACT.Copy).then_inc(gT_act, 1)

            def down(d):
                def group(g, slot_next, last=False):
                    for b in range(NB):
                        if b == 0 and isinstance(g, int) and g == 0 and d in (1, 3):
                            gT_out(FB - 1, FB * (d // 2) + FB)
                        if b == 0 and not last:
                            stationary(d, g + 1, slot_next)
                        if last and d < 3:
                            squares(d, b)
                            if b >= 1:
                                act_tiles(d, b - 1)
                        split(g + (DOWN_C[d] // 4 + 1), b)

                if DOWN_G[d] > 4:
                    group(0, act_slot(1))
                    group(1, act_slot(2))
                    with act.Fori(0, (DOWN_G[d] - 3) // 2) as i:
                        for u in range(2):
                            group(2 * i + (2 + u), act_slot(3 + u))
                else:
                    for g in range(DOWN_G[d] - 1):
                        group(g, act_slot(g + 1))
                group(DOWN_G[d] - 1, None, last=True)

            def up(f, c0, d):
                def body(i, first):
                    for c in range(8):
                        if c == 1 and first:
                            act_tiles(d, 3)
                        if c == 0 and not first:
                            gT_out(i - 1, i + FB * f)
                        if c == 3:
                            act.wait_ge(chunk_used, 8 * i + (c0 + 4))
                            if first:
                                act.wait_ge(rstd_done, d + 1)
                            for t in range(NT):
                                k = A.activation(gtmp[:, t, :], ps[t][:, :], ACT.Silu,
                                                 scale=stat(RS + 2 * (d + 1) + t))
                            k.then_inc(silu_done, 1)
                        split(2 * i + ((c0 + c + 4) // 4), c % 4)
                        if c == 5 and isinstance(i, int) and i == FB - 1:
                            stationary(d + 1, 0, act_slot(0))

                body(0, True)
                with act.Fori(1, FB - 1) as i:
                    body(i, False)
                body(FB - 1, False)

            for dst, src in vec_loads[6:]:
                act.dma_start(dst, src, allow_slow_non_contiguous=True).then_inc(vec_in, 16)
            act.wait_ge(x_rstd, 1)
            A.activation(xn[:, 0, :], h[:, 0, :], ACT.Copy, scale=stat(RS)).then_inc(xn_done, 1)
            act.wait_ge(cols_done, 3)
            act_tiles("x", 0)
            act_tiles("x", 1)
            split(0, 0)
            split(0, 1)
            act_tiles("x", 2)
            split(0, 2)
            act_tiles("x", 3)
            split(0, 3)

            def rec_hi_block(n):
                act.wait_ge(conv_done, n // 2 + 1)
                if n == 0:
                    act.wait_ge(rope_done, 1)
                    act.wait_ge(decay_done, 1)
                if n >= 4:
                    gate_block_done(act, n - 4)
                A.activation(rec_split[:, n % 4, 0, :, :], feat[:, 2 * n:2 * n + 2, :], ACT.Copy).then_inc(rec_hi, 1)

            for n in range(C_REC, C_GATE):
                j = n // 4
                if n == 1:
                    act.wait_ge(lam_done, 1)
                    A.activation(sp[:, 1, :], sp[:, 0, :], ACT.Exp, scale=-1.0).then_inc(lam_exp, 1)
                if n == 4:
                    act.wait_ge(angles_done, 1)
                    A.activation(ang[:, 5, :, :], ang[:, 2, :, :], ACT.Sin)
                    A.activation(ang[:, 6, :, :], ang[:, 2, :, :], ACT.Sin, scale=-1.0)
                    A.activation(ang[:, 7, :, :], ang[:, 4, :, :], ACT.Sin).then_inc(sin_done, 1)
                if n % 4 == 3:
                    act.wait_ge(chunk_used, n + 1)
                    if j:
                        act.wait_ge(conv_done, j)
                    for q in range(4):
                        A.activation(utmp[:, q, 3:3 + SEQ], lru_bank(j, q), ACT.Identity,
                                     bias=col(1, B_IN + KT + 4 * j + q)).then_inc(act_hi_done, 1)
                if n in (7, 11):
                    rec_hi_block(n // 4 * 2 - 2)
                    rec_hi_block(n // 4 * 2 - 1)
                split((n + 4) // 4, n % 4)
            for c in range(4):
                for n in (2 * c, 2 * c + 1):
                    gate_block_done(act, n)
                    if n >= 2:
                        act.wait_ge(ix_done, n - 1)
                    for q in range(4):
                        dst = feat[:, 16 + 2 * n + q, :] if q < 2 else gi[:, 2 * (n % 2) + q - 2, :]
                        A.activation(dst, lru_bank(4 + n, q), ACT.Sigmoid,
                                     bias=col(2, B_GATE + 4 * n + q)).then_inc(act_hi_done, 1)
                    if n + 4 < 8:
                        rec_hi_block(n + 4)
                split((C_GATE + c + 4) // 4, c)

            def decay_tiles(k0):
                act.wait_ge(act_hi_done, HI0["lru"] + 16 + 2 * k0 + 8)
                if k0 == 0:
                    act.wait_ge(decay_done, 1)
                    act.wait_ge(chunk_used, C_GEL)
                if k0 >= 8:
                    act.wait_ge(scan_done, k0 - 4)
                for k in range(k0, k0 + 4):
                    A.activation(feat[:, 32 + k % 8, :], feat[:, 16 + k, :], ACT.Exp,
                                 scale=decay[:, 0, k:k + 1]).then_inc(a_done, 1)
                act.wait_ge(a_done, k0 + 4)
                if k0:
                    act.wait_ge(z_done, k0 // 4)
                A.activation(feat[:, 40:44, :], feat[:, 32 + k0 % 8:36 + k0 % 8, :], ACT.Square)
                for k in range(k0, k0 + 4):
                    A.activation(feat[:, 16 + k, :], feat[:, 16 + k, :], ACT.Tanh,
                                 scale=decay[:, 1, k:k + 1]).then_inc(tanh_done, 1)

            def sqrt_batch(bt):
                act.wait_ge(z_done, 2 * (bt + 1))
                s8 = feat[:, 16 + 8 * bt:24 + 8 * bt, :]
                A.activation(s8, s8, ACT.Sqrt).then_inc(sqrt_done, 1)

            for s in range(16):
                n = C_GEL + s
                if s % 4 == 3:
                    j = s // 4
                    act.wait_ge(chunk_used, n + 1)
                    if j:
                        act.wait_ge(y_done, j)
                    else:
                        act.wait_ge(ix_done, 8)
                    for q in range(4):
                        A.activation(gi[:, q, :], lru_bank(12 + j, q), ACT.Gelu_apprx_tanh,
                                     bias=col(1, B_IN + 4 * j + q)).then_inc(act_hi_done, 1)
                if s == 12:
                    stationary(0, 0, act_slot(0))
                split((n + 4) // 4, s % 4)
                if s in (0, 1, 4, 5):
                    decay_tiles({0: 0, 1: 4, 4: 8, 5: 12}[s])
                if s in (2, 6):
                    sqrt_batch(s // 4)

            down(0)
            up(0, C_UP0, 0)
            down(1)

            for j in range(8):
                if j == 0:
                    act_tiles(1, 3)
                    act.wait_ge(hT_copied, 8)
                    act.wait_ge(act_lo_done, LO0[1] + 16)
                act.wait_ge(chunk_used, C_DKV + j + 1)
                for k in (2 * j, 2 * j + 1):
                    A.activation(act_hi[:, k, :], feat[:, k, :], ACT.Copy,
                                 scale=col(0, G_MIX1 + k)).then_inc(act_hi_done, 1)
                if j == 7:
                    act.wait_ge(rstd_done, 2)
                    act.wait_ge(act_lo_done, LO0["mix"] + 16)
                    for t in range(NT):
                        for hf in range(2):
                            A.activation(ckr[:, t, hf * HALF:(hf + 1) * HALF], ps[2 * hf + t][:, 0:HALF], ACT.Copy,
                                         scale=stat(RS + 4 + t)).then_inc(ckr_done, 1)
                    act.wait_ge(ckr_done, 4)
                    act.wait_ge(h_sq, 2 * NB)
                    for t in range(NT):
                        A.activation(junk[:, t, :], ckr[:, t, 0:KV_LORA], ACT.Square, accum_out=stat(SS_C + t))
                        i = A.activation(gtmp[:, t, 0:ROPE], ckr[:, t, KV_LORA:DKV], ACT.Square,
                                         accum_out=stat(SS_KR + t))
                    i.then_inc(c_sq, 1)
                split((C_DKV + j + 4) // 4, j % 4)

            def latent_hi(i, g0):
                act.wait_ge(cT_mm, i + 1)
                for q in range(LT):
                    A.activation(act_hi[:, 4 * i + q, :], latent_psum(i, q), ACT.Copy,
                                 scale=col(0, g0 + q)).then_inc(c_hi, 1)

            for j in range(4):
                if j == 2:
                    latent_hi(0, G_CKV)
                if j == 3:
                    act.wait_ge(chunk_used, C_DQ + 4)
                    act.wait_ge(c_sq, 1)
                    for t in range(NT):
                        if t:
                            act.wait_ge(cq_done, 1)
                        A.activation(junk[:, t, :], ps[4 + t][:, :], ACT.Square, scale=stat(RS + 4 + t),
                                     accum_out=stat(SS_Q + t)).then_inc(cq_sq, 1)
                split((C_DQ + j + 4) // 4, j)

            def pair(m, u, live=True, mid=True, old=True, first=False, last=False):
                p = 2 * m + u

                def values():
                    act.wait_ge(k_norm, p + 1)
                    for t in range(NT):
                        i = A.activation(v_sb[:, u, t, :, :], kv_psum(t)[:, :, NOPE:NOPE + VD], ACT.Copy)
                    i.then_inc(v_done, 1)

                if old:
                    for e in range(2):
                        act.wait_ge(s_max, 2 * p - 3 + e)
                        for t in range(NT):
                            sl = prob(e, t)
                            i = A.activation(sl, sl, ACT.Exp, bias=stat(NMX + 2 * e + t),
                                             accum_out=stat(PSUMS + 2 * e + t))
                    i.then_inc(s_exp, 1)
                if first:
                    latent_hi(1, G_CQ)
                if live:
                    act.wait_ge(chunk_used, 2 * p + (C_PAIR + 1))
                    if not first:
                        act.wait_ge(q_ss, p)
                    for t in range(NT):
                        i = A.activation(sq[:, t, :, 0:NOPE], kv_psum(t)[:, :, 0:NOPE], ACT.Square)
                    i.then_inc(k_sq, 1)
                if mid:
                    act.wait_ge(t_mm, p)
                    A.activation(knT[:, :, :].rearrange("p e s -> p (e s)"), ps[4][:, :], ACT.Copy, scale=col(0, G_KN))
                    A.activation(qnT[:, :, :].rearrange("p e s -> p (e s)"), ps[5][:, :], ACT.Copy,
                                 scale=col(0, G_QN)).then_inc(t_act, 1)
                if live:
                    split(m + (C_PAIR // 4 + 1), 2 * u)
                if old:
                    act.wait_ge(pt_mm, p - 1)
                    A.activation(pT[:, 0, :], ps[7][:, 0:3 * P], ACT.Copy).then_inc(pt_act, 1)
                if first:
                    values()
                if live:
                    act.wait_ge(chunk_used, 2 * p + (C_PAIR + 2))
                    act.wait_ge(k_ss, p + 1)
                    for t in range(NT):
                        i = A.activation(sq[:, t, :, :], q_psum(t), ACT.Square)
                    i.then_inc(q_sq, 1)
                if old:
                    act.wait_ge(o_mm, p - 1)
                    A.activation(feat[:, bass.ds(2 * p - 4, 2), :], ps[7][:, :].rearrange("p (e s) -> p e s", e=2),
                                 ACT.Copy).then_inc(o_done, 1)
                if live:
                    if not first:
                        values()
                    if last:
                        stationary(2, 0, act_slot(0))
                    split(m + (C_PAIR // 4 + 1), 2 * u + 1)

            pair(0, 0, mid=False, old=False, first=True)
            pair(0, 1, old=False)
            with act.Fori(1, PAIRS // 2 - 1) as m:
                pair(m, 0)
                pair(m, 1)
            pair(PAIRS // 2 - 1, 0)
            pair(PAIRS // 2 - 1, 1, last=True)
            pair(PAIRS // 2, 0, live=False)
            pair(PAIRS // 2, 1, live=False, mid=False)

            down(2)
            up(1, C_UP1, 2)
            down(3)

        @block.vector
        def _(dve):
            V = nc.vector

            def split(m, s):
                if isinstance(m, int) and 4 * m + s >= CHUNKS:
                    return
                size = chunk_size(4 * m + s) if isinstance(m, int) else KC * W
                dve.wait_ge(w_hi_done, 4 * m + s + 1)
                V.tensor_tensor(flat_chunk(w_lo, s, size), flat_chunk(raw, s, size),
                                flat_chunk(w_hi, s, size).bitcast(F32), ALU.subtract).then_inc(w_lo_done, 1)

            def lo_tile(k, src, g):
                return V.scalar_tensor_tensor(out=act_lo[:, k, :], in0=src, scalar=g,
                                              in1=act_hi[:, k, :].bitcast(F32), op0=ALU.mult, op1=ALU.subtract)

            def act_tiles(kind, b):
                for q in range(4):
                    k = 4 * b + q
                    if q % 2 == 0:
                        dve.wait_ge(act_hi_done, HI0[kind] + k + 2)
                        if kind == 1:
                            dve.wait_ge(hT_copied, k // 2 + 1)
                    lo_tile(k, hT_psum(b, q), col(0, gain[kind] + k)).then_inc(act_lo_done, 1)

            def update(d, b):
                dve.wait_ge(chunk_used, DOWN_C[d] + 4 * (DOWN_G[d] - 1) + b + 1)
                if d == 0 and b == 0:
                    dve.wait_ge(bout_added, 1)
                for t in range(NT):
                    hb = h[:, t, b * W:(b + 1) * W]
                    i = V.tensor_tensor(hb, hb, ps[2 * b + t][:, :], ALU.add)
                i.then_inc(h_done, 1)

            def stationary(g, slot, n):
                dve.wait_ge(st_hi, n)
                V.tensor_tensor(act_lo[:, slot:slot + 4, :], feat[:, bass.ds(4 * g, 4), :],
                                act_hi[:, slot:slot + 4, :].bitcast(F32), ALU.subtract).then_inc(st_lo, 1)

            def gT_out(i, n):
                dve.wait_ge(gT_mm, n)
                V.tensor_copy(feat[:, bass.ds(4 * i + 2, 2), :],
                              ps[5][:, :].rearrange("p (a b) -> p a b", a=2)).then_inc(gT_dve, 1)

            def down(d):
                def group(g, slot_next, last=False):
                    for b in range(NB):
                        if b == 0 and isinstance(g, int) and g == 0 and d in (1, 3):
                            gT_out(FB - 1, FB * (d // 2) + FB)
                        if b == 0 and not last:
                            stationary(g + 1, slot_next, g + (DOWN_G0[d] + 2))
                        if last:
                            update(d, b)
                            if d < 3 and b >= 1:
                                act_tiles(d, b - 1)
                        split(g + (DOWN_C[d] // 4 + 1), b)

                if DOWN_G[d] > 4:
                    group(0, act_slot(1))
                    group(1, act_slot(2))
                    with dve.Fori(0, (DOWN_G[d] - 3) // 2) as i:
                        for u in range(2):
                            group(2 * i + (2 + u), act_slot(3 + u))
                else:
                    for g in range(DOWN_G[d] - 1):
                        group(g, act_slot(g + 1))
                group(DOWN_G[d] - 1, None, last=True)
                if d < 3:
                    dve.wait_ge(h_sq, NB * (d + 1))
                    if d:
                        dve.wait_ge(rstd_done, d)
                    V.tensor_reduce(stat(SS_T, 2), stat(SS_D, NT * NB).rearrange("p (t b) -> p t b", t=NT),
                                    AX.X, ALU.add).then_inc(ms_done, 1)

            def up(f, c0, d):
                def body(i, first):
                    for c in range(8):
                        if c == 1 and first:
                            act_tiles(d, 3)
                        if c == 0 and not first:
                            gT_out(i - 1, i + FB * f)
                        if c == 7:
                            dve.wait_ge(chunk_used, 8 * i + (c0 + 8))
                            dve.wait_ge(silu_done, i + (FB * f + 1))
                            for t in range(NT):
                                k = V.scalar_tensor_tensor(out=gtmp[:, t, :], in0=ps[2 + t][:, :],
                                                           scalar=stat(RS + 2 * (d + 1) + t), in1=gtmp[:, t, :],
                                                           op0=ALU.mult, op1=ALU.mult)
                            k.then_inc(g_done, 1)
                        if c == 6 and isinstance(i, int) and i == FB - 1:
                            stationary(0, act_slot(0), DOWN_G0[d + 1] + 1)
                        split(2 * i + ((c0 + c + 4) // 4), c % 4)

                body(0, True)
                with dve.Fori(1, FB - 1) as i:
                    body(i, False)
                body(FB - 1, False)

            n_prep = [0]

            def step(ins):
                n_prep[0] += 1
                ins.then_inc(prep, 1)
                dve.wait_ge(prep, n_prep[0])

            for t in range(NT):
                dve.wait_ge(x_in[t], 16)
                V.tensor_tensor_reduce(xn[:, t, :], h[:, t, :], h[:, t, :], 1.0, 0.0, ALU.mult, ALU.add,
                                       stat(SS_X + t)).then_inc(x_sq, 1)

            def reduce_angle(dst, tmp, shift, quarter):
                r, n = ang[:, dst, :, :], ang[:, tmp, :, :]
                step(V.tensor_scalar(r, ang[:, 0, :, :], float(1 / (2 * np.pi)), shift, ALU.mult, ALU.add))
                step(V.tensor_scalar(n, r, 12582912.0, None, ALU.add))
                step(V.tensor_scalar(n, n, -12582912.0, None, ALU.add))
                step(V.scalar_tensor_tensor(out=r, in0=n, scalar=-TWO_PI[0], in1=ang[:, 0, :, :],
                                            op0=ALU.mult, op1=ALU.add))
                for part in TWO_PI[1:]:
                    step(V.scalar_tensor_tensor(out=r, in0=n, scalar=-part, in1=r, op0=ALU.mult, op1=ALU.add))
                step(V.tensor_scalar(r, r, quarter, PI_DOWN, ALU.add, ALU.min))
                step(V.tensor_scalar(r, r, -PI_DOWN, None, ALU.max))

            dve.wait_ge(x_rstd, 2)
            V.tensor_scalar(xn[:, 1, :], h[:, 1, :], stat(RS + 1), None, ALU.mult).then_inc(xn_done, 1)
            for r, n_rows in enumerate((ROWS_A, ROWS_B, ROWS_C)):
                dve.wait_ge(cols_mm, r + 1)
                V.tensor_copy(cols[:, r, 0:n_rows], ps[7 - r][:, 0:n_rows]).then_inc(cols_done, 1)
            act_tiles("x", 0)
            act_tiles("x", 1)
            split(0, 0)
            split(0, 1)
            act_tiles("x", 2)
            split(0, 2)
            act_tiles("x", 3)
            split(0, 3)

            def rec_lo_block(n):
                dve.wait_ge(rec_hi, n + 1)
                V.tensor_tensor(rec_split[:, n % 4, 1, :, :], feat[:, 2 * n:2 * n + 2, :],
                                rec_split[:, n % 4, 0, :, :].bitcast(F32), ALU.subtract).then_inc(rec_lo, 1)

            def convolve(j):
                for w in (3, 2, 1, 0):
                    for q in range(4):
                        k = 4 * j + q
                        tap = col(1, CONV_W + KT * w + k)
                        src, dst = utmp[:, q, w:w + SEQ], feat[:, k, :]
                        if w == 3:
                            dve.wait_ge(act_hi_done, HI0["lru"] + k + 1)
                            i = V.tensor_scalar(dst, src, tap, col(1, CONV_B + k), ALU.mult, ALU.add)
                        else:
                            dve.wait_ge(conv_step, 12 * j + 4 * (2 - w) + q + 1)
                            i = V.scalar_tensor_tensor(out=dst, in0=src, scalar=tap, in1=dst,
                                                       op0=ALU.mult, op1=ALU.add)
                        if w:
                            i.then_inc(conv_step, 1)
                i.then_inc(conv_done, 1)

            for n in range(C_REC, C_GATE):
                if n == 0:
                    dve.wait_ge(cols_done, 3)
                    step(V.scalar_tensor_tensor(out=sp[:, 0, :], in0=cols[:, 2, LAM:LAM + KT], scalar=-1.0,
                                                in1=cols[:, 2, LAM:LAM + KT], op0=ALU.mult, op1=ALU.max))
                    V.tensor_scalar(sp[:, 2, :], cols[:, 2, LAM:LAM + KT], -1.0, 0.0, ALU.mult,
                                    ALU.max).then_inc(lam_done, 1)
                if n == 1:
                    dve.wait_ge(lam_exp, 1)
                    y, s1, s2, q1 = sp[:, 1, :], sp[:, 3, :], sp[:, 4, :], sp[:, 5, :]
                    step(V.tensor_scalar(s1, y, 2.0, None, ALU.add))
                    step(V.reciprocal(s1, s1))
                    step(V.tensor_tensor(s1, s1, y, ALU.mult))
                    step(V.tensor_tensor(s2, s1, s1, ALU.mult))
                    step(V.tensor_scalar(q1, s2, 1.0 / 15, None, ALU.mult))
                    for c in (13, 11, 9, 7, 5, 3):
                        step(V.scalar_tensor_tensor(out=q1, in0=q1, scalar=1.0 / c, in1=s2, op0=ALU.add, op1=ALU.mult))
                    step(V.scalar_tensor_tensor(out=q1, in0=q1, scalar=1.0, in1=s1, op0=ALU.add, op1=ALU.mult))
                    step(V.scalar_tensor_tensor(out=q1, in0=q1, scalar=2.0, in1=sp[:, 2, :], op0=ALU.mult, op1=ALU.add))
                    V.tensor_scalar(decay[:, 0, :], q1, -8.0, None, ALU.mult)
                    V.tensor_scalar(decay[:, 1, :], q1, 8.0, None, ALU.mult).then_inc(decay_done, 1)
                if n == 2:
                    dve.wait_ge(rope_in, ROPE_ALL)
                    step(V.tensor_copy(posf[:, :], posi[:, :]))
                    for t in range(NT):
                        step(V.tensor_scalar(ang[:, 0, t, :], invf[:, :], posf[:, t:t + 1], None, ALU.mult))
                    reduce_angle(2, 1, 0.0, 0.0)
                    reduce_angle(4, 3, 0.25, float(np.pi / 2))
                    V.tensor_copy(posf[:, :], posi[:, :]).then_inc(angles_done, 1)
                if n % 4 == 3:
                    convolve(n // 4)
                if n in (7, 11):
                    rec_lo_block(n // 4 * 2 - 2)
                    rec_lo_block(n // 4 * 2 - 1)
                split((n + 4) // 4, n % 4)
            for c in range(4):
                for n in (2 * c, 2 * c + 1):
                    if n + 4 < 8:
                        rec_lo_block(n + 4)
                split((C_GATE + c + 4) // 4, c)

            def gain_of_input(hb):
                t4 = feat[:, 16 + 4 * hb:20 + 4 * hb, :]
                dve.wait_ge(tanh_done, 4 * hb + 4)
                V.scalar_tensor_tensor(out=t4, in0=feat[:, 40:44, :], scalar=1.0, in1=t4, op0=ALU.add,
                                       op1=ALU.mult).then_inc(z_step, 1)
                dve.wait_ge(z_step, hb + 1)
                V.tensor_scalar(t4, t4, 1e-34, None, ALU.max).then_inc(z_done, 1)

            def scans(bt):
                dve.wait_ge(sqrt_done, bt + 1)
                dve.wait_ge(ix_done, 4 * (bt + 1))
                s8 = feat[:, 16 + 8 * bt:24 + 8 * bt, :]
                V.tensor_tensor(s8, s8, feat[:, 8 * bt:8 * bt + 8, :], ALU.mult).then_inc(b_done, 1)
                dve.wait_ge(b_done, bt + 1)
                for k in range(8 * bt, 8 * bt + 8):
                    V.tensor_tensor_scan(feat[:, k, :], feat[:, 32 + k % 8, :], feat[:, 16 + k, :], 0.0,
                                         ALU.mult, ALU.add).then_inc(scan_done, 1)

            for s in range(16):
                n = C_GEL + s
                if s in (1, 2, 5, 6):
                    gain_of_input({1: 0, 2: 1, 5: 2, 6: 3}[s])
                if s in (3, 7):
                    scans(s // 4)
                if s % 4 == 3:
                    j = s // 4
                    dve.wait_ge(act_hi_done, HI0["lru"] + 48 + 4 * (j + 1))
                    dve.wait_ge(scan_done, 4 * (j + 1))
                    y4 = feat[:, 4 * j:4 * j + 4, :]
                    V.tensor_tensor(y4, y4, gi[:, :, :], ALU.mult).then_inc(y_done, 1)
                if s == 12:
                    stationary(0, act_slot(0), 1)
                split((n + 4) // 4, s % 4)

            down(0)
            up(0, C_UP0, 0)
            down(1)

            for j in range(8):
                if j == 0:
                    act_tiles(1, 3)
                for k in (2 * j, 2 * j + 1):
                    dve.wait_ge(act_hi_done, HI0["mix"] + k + 1)
                    lo_tile(k, feat[:, k, :], col(0, G_MIX1 + k)).then_inc(act_lo_done, 1)
                if j < 7:
                    split((C_DKV + j + 4) // 4, j % 4)
            dve.wait_ge(ckr_done, 4)
            dve.wait_ge(rope_done, 1)
            kraw = ckr[:, :, KV_LORA:DKV]
            V.tensor_tensor(rot_k[:, :, 0:32], kraw[:, :, 32:64], rope_s[:, 0, :, 0:32], ALU.mult)
            V.tensor_tensor(rot_k[:, :, 32:64], kraw[:, :, 0:32], rope_s[:, 0, :, 32:64], ALU.mult)
            V.tensor_tensor(kr_all[:, :, :], kraw, rope_c[:, 0, :, :], ALU.mult).then_inc(kr_step, 1)
            dve.wait_ge(kr_step, 1)
            V.tensor_tensor(kr_all[:, :, :], kr_all[:, :, :], rot_k[:, :, :], ALU.add).then_inc(kr_step, 1)
            dve.wait_ge(kr_step, 2)

            def latent_norm(i, buf, rs):
                dve.wait_ge(c_rstd, i + 1)
                for t in range(NT):
                    k = V.tensor_scalar(buf[:, t, 0:KV_LORA], buf[:, t, 0:KV_LORA], stat(rs + t), None, ALU.mult)
                k.then_inc(c_norm, 1)

            def latent_lo(i, g0):
                for q in range(LT):
                    if q % 2 == 0:
                        dve.wait_ge(c_hi, LT * i + q + 2)
                    lo_tile(4 * i + q, latent_psum(i, q), col(0, g0 + q)).then_inc(c_lo, 1)

            latent_norm(0, ckr, RS_C)
            split((C_DKV + 7 + 4) // 4, 3)
            for j in range(4):
                if j == 2:
                    latent_lo(0, G_CKV)
                if j == 3:
                    dve.wait_ge(chunk_used, C_DQ + 4)
                    for t in (1, 0):
                        if t == 0:
                            dve.wait_ge(cq_sq, 1)
                        V.tensor_scalar(cq[:, t, :], ps[4 + t][:, :], stat(RS + 4 + t), None,
                                        ALU.mult).then_inc(cq_done, 1)
                    dve.wait_ge(cq_done, 2)
                    latent_norm(1, cq, RS_Q)
                split((C_DQ + j + 4) // 4, j)

            def pair(m, u, live=True, mid=True, old=True, last=False):
                p = 2 * m + u
                if old:
                    dve.wait_ge(s_mm, p - 1)
                    V.memset(stat(WAIT_SLOT), 0.0)
                    for e in range(2):
                        for t in range(NT):
                            i = V.tensor_tensor_reduce(prob(e, t), score_psum(e, t), mask_of(t), SCALE, -3e38,
                                                       ALU.add, ALU.max, stat(MX + 2 * e + t))
                        i.then_inc(s_step, 1)
                        dve.wait_ge(s_step, 3 * p - 5 + e)
                        V.tensor_scalar(stat(NMX + 2 * e, 2), stat(MX + 2 * e, 2), -1.0, None,
                                        ALU.mult).then_inc(s_max, 1)
                if old:
                    dve.wait_ge(s_exp, p - 1)
                    V.reciprocal(stat(RPS, 4), stat(PSUMS, 4)).then_inc(s_step, 1)
                    dve.wait_ge(s_step, 3 * p - 3)
                    for e in range(2):
                        for t in range(NT):
                            i = V.tensor_scalar(prob(e, t), prob(e, t), stat(RPS + 2 * e + t), None, ALU.mult)
                    i.then_inc(p_done, 1)
                if mid:
                    dve.wait_ge(t_mm, p)
                    V.tensor_copy(krT[:, :], ps[6][:, 0:SEQ])
                    for e in range(2):
                        rows_e = slice(e * ROPE, (e + 1) * ROPE)
                        i = V.tensor_copy(qrT[rows_e, e, :], ps[6][rows_e, SEQ:2 * SEQ])
                    i.then_inc(t_dve, 1)
                if live and not mid:
                    latent_lo(1, G_CQ)
                if live:
                    dve.wait_ge(k_sq, p + 1)
                    V.tensor_reduce(stat(SS_K, 4), sq[:, :, :, 0:NOPE], AX.X, ALU.add).then_inc(k_ss, 1)
                if old:
                    dve.wait_ge(pt_mm, p - 1)
                    V.tensor_copy(pT[:, 1, :], ps[6][:, 0:3 * P]).then_inc(pt_dve, 1)
                if isinstance(m, int) and p == PAIRS:
                    split(C_WO // 4, 2)
                if mid:
                    split(m + (C_PAIR // 4 + (u + 1) // 2), (2 * u + 3) % 4)
                if live:
                    dve.wait_ge(k_rs, p + 1)
                    for t in range(NT):
                        rs = stat(RS_K + 2 * t, 2)[:, :, None]
                        V.tensor_tensor(kn[:, t, :, :], kv_psum(t)[:, :, 0:NOPE], rs.broadcast_to([P, 2, NOPE]),
                                        ALU.mult)
                        i = V.tensor_tensor(kr[:, t, :, :], kr_all[:, t, None, :].broadcast_to([P, 2, ROPE]),
                                            rs.broadcast_to([P, 2, ROPE]), ALU.mult)
                    i.then_inc(k_norm, 1)
                if live:
                    dve.wait_ge(q_sq, p + 1)
                    V.tensor_reduce(stat(SS_QH, 4), sq[:, :, :, :], AX.X, ALU.add).then_inc(q_ss, 1)
                    if last:
                        stationary(0, act_slot(0), DOWN_G0[2] + 1)
                    else:
                        split(m + (C_PAIR // 4 + 1), 2 * u)
                    dve.wait_ge(q_rs, p + 1)
                    for t in range(NT):
                        rs = stat(RS_QH + 2 * t, 2)[:, :, None]
                        i = V.tensor_tensor(qn[:, t, :, :], q_psum(t), rs.broadcast_to([P, 2, QK]), ALU.mult)
                    i.then_inc(q_step, 1)
                    dve.wait_ge(q_step, 2 * p + 1)
                    for t in range(NT):
                        sn = rope_s[:, 1, t, None, :].broadcast_to([P, 2, ROPE])
                        cs = rope_c[:, 1, t, None, :].broadcast_to([P, 2, ROPE])
                        V.tensor_tensor(rot[:, t, :, 0:32], qn[:, t, :, NOPE + 32:QK], sn[:, :, 0:32], ALU.mult)
                        V.tensor_tensor(rot[:, t, :, 32:64], qn[:, t, :, NOPE:NOPE + 32], sn[:, :, 32:64], ALU.mult)
                        i = V.tensor_tensor(qr[:, t, :, :], qn[:, t, :, NOPE:QK], cs, ALU.mult)
                    i.then_inc(q_step, 1)
                    dve.wait_ge(q_step, 2 * p + 2)
                    V.tensor_tensor(qr[:, :, :, :].rearrange("p t e d -> p (t e d)"),
                                    qr[:, :, :, :].rearrange("p t e d -> p (t e d)"),
                                    rot[:, :, :, :].rearrange("p t e d -> p (t e d)"), ALU.add).then_inc(q_norm, 1)

            pair(0, 0, mid=False, old=False)
            pair(0, 1, old=False)
            with dve.Fori(1, PAIRS // 2 - 1) as m:
                pair(m, 0)
                pair(m, 1)
            pair(PAIRS // 2 - 1, 0)
            pair(PAIRS // 2 - 1, 1, last=True)
            pair(PAIRS // 2, 0, live=False)
            pair(PAIRS // 2, 1, live=False, mid=False)

            down(2)
            up(1, C_UP1, 2)
            down(3)

        @block.gpsimd
        def _(pool):
            G = nc.gpsimd
            n_pool = [0]

            def step(ins):
                n_pool[0] += 1
                ins.then_inc(pool_step, 1)
                pool.wait_ge(pool_step, n_pool[0])

            for dst, src in rope_in_loads:
                pool.dma_start(dst, src, allow_slow_non_contiguous=True).then_inc(rope_in, 16)
            pool.dma_start(bout[:, :], a["lru_b_out"][0:1, :].broadcast_to([P, D])).then_inc(bout_in, 16)
            G.memset(minus_half[:, :], -0.5)
            G.memset(stat(QK_EPS4, 4), QK * EPS)
            G.memset(stat(INV_QK4, 4), 1.0 / QK)
            G.memset(utmp[:, :, 0:3], 0.0)
            G.memset(ident[:, :], 0.0)
            step(G.memset(mask[:, :], 0.0))
            G.affine_select(out=ident[:, :], in_=ident[:, :], compare_op=ALU.not_equal, fill=1.0, base=0,
                            pattern=[[-1, P]], channel_multiplier=1)
            for c in (0, 2):
                tri = mask[:, c * P:(c + 1) * P]
                i = G.affine_select(out=tri, in_=tri, compare_op=ALU.is_ge, fill=NEG, base=0,
                                    pattern=[[-1, P]], channel_multiplier=1)
            i.then_inc(consts, 1)

            def rstd(ss, rs, n, width, signal):
                step(G.tensor_scalar(stat(rs, n), stat(ss, n), 1.0 / width, EPS, ALU.mult, ALU.add))
                G.tensor_tensor(stat(rs, n), stat(rs, n), minus_half[:, 0:n], ALU.pow).then_inc(signal, 1)

            for t in range(NT):
                pool.wait_ge(x_sq, t + 1)
                rstd(SS_X + t, RS + t, 1, D, x_rstd)
            pool.wait_ge(bout_in, 16)
            pool.wait_ge(xn_done, 2)
            for t in range(NT):
                i = G.tensor_tensor(h[:, t, :], h[:, t, :], bout[:, :], ALU.add)
            i.then_inc(bout_added, 1)
            pool.wait_ge(sin_done, 1)
            for kind in range(2):
                for t in range(NT):
                    for half in range(2):
                        cut = slice(32 * half, 32 * half + 32)
                        other = slice(32 - 32 * half, 64 - 32 * half)
                        G.tensor_tensor(rope_c[:, kind, t, cut], ang[:, 7, t, :], rope_g[:, kind, cut], ALU.mult)
                        i = G.tensor_tensor(rope_s[:, kind, t, cut], ang[:, 6 - half, t, :], rope_g[:, kind, other],
                                            ALU.mult)
            i.then_inc(rope_done, 1)
            for n in range(8):
                pool.wait_ge(act_hi_done, HI0["lru"] + 16 + 4 * (n + 1))
                G.tensor_tensor(feat[:, 2 * n:2 * n + 2, :], feat[:, 2 * n:2 * n + 2, :],
                                gi[:, 2 * (n % 2):2 * (n % 2) + 2, :], ALU.mult).then_inc(ix_done, 1)
            for d in (0, 1):
                pool.wait_ge(ms_done, d + 1)
                rstd(SS_T, RS + 2 * (d + 1), 2, D, rstd_done)
            pool.wait_ge(st_lo, DOWN_G0[2])
            pool.wait_ge(rstd_done, 2)
            step(G.memset(qrT[ROPE:P, 0, :], 0.0))
            step(G.memset(qrT[0:ROPE, 1, :], 0.0))
            G.memset(stat(POOL_SLOT), 0.0).then_inc(qz_done, 1)
            pool.wait_ge(c_sq, 1)
            rstd(SS_C, RS_C, 2, KV_LORA, c_rstd)
            for t in range(NT):
                for e in range(2):
                    step(G.tensor_scalar(stat(SS_KR4 + 2 * t + e), stat(SS_KR + t), 1.0, QK * EPS, ALU.mult, ALU.add))
            pool.wait_ge(cq_sq, 2)
            rstd(SS_Q, RS_Q, 2, Q_LORA, c_rstd)
            with pool.Fori(0, PAIRS) as p:
                for n, (ss_ready, ss, more, rs, signal) in enumerate((
                        (k_ss, SS_K, SS_KR4, RS_K, k_rs), (q_ss, SS_QH, QK_EPS4, RS_QH, q_rs))):
                    pool.wait_ge(ss_ready, p + 1)
                    G.tensor_tensor(stat(rs, 4), stat(ss, 4), stat(more, 4), ALU.add).then_inc(pair_step, 1)
                    pool.wait_ge(pair_step, 4 * p + (2 * n + 1))
                    G.tensor_tensor(stat(rs, 4), stat(rs, 4), stat(INV_QK4, 4), ALU.mult).then_inc(pair_step, 1)
                    pool.wait_ge(pair_step, 4 * p + (2 * n + 2))
                    G.tensor_tensor(stat(rs, 4), stat(rs, 4), minus_half[:, 0:4], ALU.pow).then_inc(signal, 1)
            pool.wait_ge(ms_done, 3)
            rstd(SS_T, RS + 6, 2, D, rstd_done)

        @block.tensor
        def _(pe):
            T = nc.tensor

            def products(outs, k, t_of, s, kk, c0, width, first, last):
                for t in range(NT):
                    hi, lo = (buf[:, k, t * P:(t + 1) * P] for buf in (act_hi, act_lo))
                    passes = ((hi, w_hi), (hi, w_lo), (lo, w_hi))
                    for n, (x_part, w_part) in enumerate(passes):
                        wp = t_of(w_part, s, kk)[:, c0:c0 + width]
                        i = T.matmul(outs[t], x_part, wp, start=first and n == 0, stop=last and n == 2)
                return i

            def chunk_rows(buf, s, kk):
                return buf[:, s, kk, :]

            def chunk(m, s, outs, k0, first, last, width=W, rows_of=chunk_rows, between=None, at=2):
                pe.wait_ge(w_lo_done, 4 * m + s + 1)
                for kk in range(KC):
                    if kk == at and between:
                        between()
                    i = products(outs, k0 + kk, rows_of, s, kk, 0, width, first and kk == 0, last and kk == KC - 1)
                i.then_inc(chunk_used, 1)

            def transpose_h(d, b):
                pe.wait_ge(h_done, d * NB + b + 1)
                for q in range(4):
                    for t in range(NT):
                        k = 4 * b + q
                        i = T.transpose(hT_psum(b, q)[:, t * P:(t + 1) * P], h[:, t, k * P:(k + 1) * P], ident[:, :])
                i.then_inc(hT_mm, 1)

            def down_block(d, g, slot, b, first=False, last=False, between=None):
                if b == 0:
                    pe.wait_ge(st_lo, g + (DOWN_G0[d] + 1))
                if first:
                    if d == 0:
                        pe.wait_ge(act_hi_done, HI0[0] - 4 * (b < 2))
                    elif d in (1, 3) and b == 0:
                        pe.wait_ge(silu_done, FB * (d // 2 + 1))
                    elif d in (1, 3) and b == 1:
                        pe.wait_ge(g_done, FB * (d // 2 + 1))
                    elif d in (1, 3) and b == 2:
                        pe.wait_ge(gT_act, FB * (d // 2 + 1))
                        pe.wait_ge(gT_dve, FB * (d // 2 + 1))
                    elif d == 2 and b == 0:
                        pe.wait_ge(v_done, PAIRS)
                    elif d == 2 and b == 1:
                        pe.wait_ge(q_norm, PAIRS)
                    elif d == 2 and b == 2:
                        pe.wait_ge(s_max, 2 * PAIRS)
                    elif d == 2 and b == 3:
                        pe.wait_ge(o_done, PAIRS)
                chunk(g + DOWN_C[d] // 4, b, (ps[2 * b][:, :], ps[2 * b + 1][:, :]), slot, first, last,
                      between=between)
                if first and b == 0 and d in (1, 3):
                    transpose_g(FB * (d // 2) + FB)
                if last and d < 3 and b >= 1:
                    transpose_h(d, b - 1)

            def down(d):
                def group(g, slot, first=False, last=False):
                    for b in range(NB):
                        down_block(d, g, slot, b, first, last)

                if d != 2:
                    group(0, act_slot(0), first=True)
                if DOWN_G[d] > 4:
                    group(1, act_slot(1))
                    with pe.Fori(0, (DOWN_G[d] - 3) // 2) as i:
                        for u in range(2):
                            group(2 * i + (2 + u), act_slot(2 + u))
                else:
                    for g in range(1, DOWN_G[d] - 1):
                        group(g, act_slot(g))
                group(DOWN_G[d] - 1, act_slot(DOWN_G[d] - 1), last=True)

            def transpose_g(n):
                pe.wait_ge(g_done, n)
                for q in range(4):
                    for t in range(NT):
                        i = T.transpose(ps[4 + q // 2][:, (q % 2) * SEQ + t * P:(q % 2) * SEQ + (t + 1) * P],
                                        gtmp[:, t, q * P:(q + 1) * P], ident[:, :])
                i.then_inc(gT_mm, 1)

            def up(f, c0, d):
                def body(i, first):
                    for c in range(8):
                        if first and c < 4:
                            pe.wait_ge(act_lo_done, LO0[d] + 4 * (c + 1))
                        if c == 0 and not first:
                            pe.wait_ge(silu_done, i + FB * f)
                        if c == 4 and not first:
                            pe.wait_ge(g_done, i + FB * f)
                        bank = 2 * (c // 4)
                        chunk(2 * i + ((c0 + c) // 4), c % 4, (ps[bank][:, :], ps[bank + 1][:, :]), 4 * (c % 4),
                              c % 4 == 0, c % 4 == 3)
                        if c == 1 and first:
                            transpose_h(d, 3)
                        if c == 0 and not first:
                            transpose_g(i + FB * f)

                body(0, True)
                with pe.Fori(1, FB) as i:
                    body(i, False)

            pe.wait_ge(consts, 1)
            pe.wait_ge(vec_in, VEC_ALL)
            for r, n_rows in enumerate((ROWS_A, ROWS_B, ROWS_C)):
                T.transpose(ps[7 - r][:, 0:n_rows], rows[0:n_rows, r, :],
                            ident[0:n_rows, 0:n_rows]).then_inc(cols_mm, 1)
            pe.wait_ge(xn_done, 2)
            for k in range(KT):
                if k == 10:
                    pe.wait_ge(cols_done, 3)
                for t in range(NT):
                    i = T.transpose(hT_psum(k // 4, k % 4)[:, t * P:(t + 1) * P], xn[:, t, k * P:(k + 1) * P],
                                    ident[:, :])
                if k % 2:
                    i.then_inc(xT_mm, 1)

            def lru_tiles(idx, s, kks, move, first, last):
                for kk in kks:
                    x_hi, x_lo = move(kk)
                    for q in range(4):
                        wh, wl = (buf[:, s, kk, q * P:(q + 1) * P] for buf in (w_hi, w_lo))
                        for n, (w_part, x_part) in enumerate(((wh, x_hi), (wh, x_lo), (wl, x_hi))):
                            i = T.matmul(lru_bank(idx, q), w_part, x_part, start=first and kk == kks[0] and n == 0,
                                         stop=last and kk == kks[-1] and n == 2)
                return i

            def in_block(idx, m, first):
                for s in range(4):
                    if first:
                        pe.wait_ge(act_lo_done, max(8, 4 * (s + 1)))
                    pe.wait_ge(w_lo_done, 4 * m + s + 1)
                    lru_tiles(idx, s, range(4), lambda kk: (act_hi[:, 4 * s + kk, :], act_lo[:, 4 * s + kk, :]),
                              s == 0, s == 3).then_inc(chunk_used, 1)

            for j in range(NB):
                if j >= 2:
                    pe.wait_ge(act_hi_done, HI0["lru"] + 4 * (j - 1))
                in_block(j, j, j == 0)
            for n in range(8):
                pe.wait_ge(act_hi_done, HI0["lru"] + 4 * (n + 3))
                pe.wait_ge(rec_lo, n + 1)
                pe.wait_ge(w_lo_done, C_GATE + n // 2 + 1)
                kks = (2 * (n % 2), 2 * (n % 2) + 1)
                i = lru_tiles(4 + n, n // 2, kks, lambda kk: (rec_split[:, n % 4, 0, kk % 2, :],
                                                              rec_split[:, n % 4, 1, kk % 2, :]), True, True)
                i.then_inc(chunk_used if n % 2 else gate_half, 1)
            with pe.Fori(0, NB // 2) as j2:
                for u in range(2):
                    pe.wait_ge(act_hi_done, 8 * j2 + (HI0["lru"] + 4 * (11 + u)))
                    in_block(u, 2 * j2 + (C_GEL // 4 + u), False)

            down(0)
            up(0, C_UP0, 0)
            down(1)

            for j in range(8):
                pe.wait_ge(act_lo_done, LO0[1] + max(8, 4 * (j // 2 + 1)))
                pe.wait_ge(w_lo_done, C_DKV + j + 1)
                for kk in range(2):
                    for hf in range(2):
                        def dkv_rows(buf, s, r):
                            return flat_chunk(buf, s, 2 * DKV)[:, r * DKV:(r + 1) * DKV]
                        i = products((ps[2 * hf][:, 0:HALF], ps[2 * hf + 1][:, 0:HALF]), 2 * j + kk, dkv_rows, j % 4,
                                     kk, hf * HALF, HALF, j + kk == 0, j == 7 and kk == 1)
                i.then_inc(chunk_used, 1)
                if j == 0:
                    transpose_h(1, 3)

            def transpose_latent(i, buf):
                pe.wait_ge(c_norm, i + 1)
                for q in range(LT):
                    for t in range(NT):
                        k = T.transpose(latent_psum(i, q)[:, t * P:(t + 1) * P], buf[:, t, q * P:(q + 1) * P],
                                        ident[:, :])
                k.then_inc(cT_mm, 1)

            for j in range(4):
                pe.wait_ge(act_lo_done, LO0["mix"] + 4 * (j + 1))
                chunk(C_DQ // 4, j, (ps[4][:, :], ps[5][:, :]), 4 * j, j == 0, j == 3)
                if j == 2:
                    transpose_latent(0, ckr)

            def q_rows(buf, s, kk):
                return flat_chunk(buf, s, KC * 2 * QK)[:, kk * 2 * QK:(kk + 1) * 2 * QK]

            def transpose_heads(p, old):
                pe.wait_ge(q_norm, p)
                if old:
                    pe.wait_ge(s_max, 2 * p - 2)
                for e in range(2):
                    for t in range(NT):
                        sl = slice(e * SEQ + t * P, e * SEQ + (t + 1) * P)
                        T.transpose(ps[4][:, sl], kn[:, t, e, :], ident[:, :])
                        T.transpose(ps[5][:, sl], qn[:, t, e, 0:NOPE], ident[:, :])
                for t in range(NT):
                    T.transpose(ps[6][:, t * P:(t + 1) * P], kr[:, t, :, :].rearrange("p e d -> p (e d)"),
                                ident[:, :])
                    i = T.transpose(ps[6][:, SEQ + t * P:SEQ + (t + 1) * P],
                                    qr[:, t, :, :].rearrange("p e d -> p (e d)"), ident[:, :])
                i.then_inc(t_mm, 1)

            def transpose_probs(p, mid=True):
                pe.wait_ge(p_done, p - 1)
                if mid:
                    pe.wait_ge(t_dve, p)
                for e in range(2):
                    for c in range(3):
                        i = T.transpose(ps[7 - e][:, c * P:(c + 1) * P], probs[:, e, c * P:(c + 1) * P], ident[:, :])
                i.then_inc(pt_mm, 1)

            def attend(p, u):
                pe.wait_ge(pt_act, p - 1)
                pe.wait_ge(pt_dve, p - 1)
                for e in range(2):
                    T.matmul(ps[7][:, e * SEQ:(e + 1) * SEQ], v_sb[:, u, 0, e, :], pT[:, e, 0:SEQ],
                             start=True, stop=False)
                    i = T.matmul(ps[7][:, e * SEQ + P:(e + 1) * SEQ], v_sb[:, u, 1, e, :], pT[:, e, SEQ:3 * P],
                                 start=False, stop=True)
                i.then_inc(o_mm, 1)

            def scores(p):
                pe.wait_ge(t_act, p)
                pe.wait_ge(t_dve, p)
                if isinstance(p, int) and p == 1:
                    pe.wait_ge(qz_done, 1)
                for e in range(2):
                    for t in range(NT):
                        queries, keys = slice(t * P, (t + 1) * P), slice(0, (t + 1) * P)
                        T.matmul(score_psum(e, t), qnT[:, e, queries], knT[:, e, keys], start=True, stop=False)
                        i = T.matmul(score_psum(e, t), qrT[:, e, queries], krT[:, keys], start=False, stop=True)
                i.then_inc(s_mm, 1)

            def pair(m, u, mid=True, old=True):
                p = 2 * m + u
                if mid:
                    pe.wait_ge(v_done, p)
                    pe.wait_ge(k_norm, p)
                else:
                    pe.wait_ge(ckr_done, 4)
                    pe.wait_ge(c_lo, LT)
                chunk(m + C_PAIR // 4, 2 * u, (ps[0][:, :], ps[1][:, :]), 0, True, True,
                      between=None if mid else lambda: transpose_latent(1, cq), at=3)
                if mid:
                    transpose_heads(p, old)
                else:
                    pe.wait_ge(c_lo, 2 * LT)
                chunk(m + C_PAIR // 4, 2 * u + 1, (ps[2][:, 0:2 * QK], ps[3][:, 0:2 * QK]), LT, True, True,
                      2 * QK, q_rows, between=(lambda: transpose_probs(p)) if old else None)
                if old:
                    attend(p, u)
                if mid:
                    scores(p)

            pair(0, 0, mid=False, old=False)
            pair(0, 1, old=False)
            with pe.Fori(1, PAIRS // 2) as m:
                pair(m, 0)
                pair(m, 1)
            down_block(2, 0, act_slot(0), 0, first=True)
            transpose_heads(PAIRS, True)
            transpose_probs(PAIRS)
            scores(PAIRS)
            attend(PAIRS, 0)
            down_block(2, 0, act_slot(0), 1, first=True)
            transpose_probs(PAIRS + 1, mid=False)
            down_block(2, 0, act_slot(0), 2, first=True, between=lambda: attend(PAIRS + 1, 1))
            down_block(2, 0, act_slot(0), 3, first=True)
            down(2)
            up(1, C_UP1, 2)
            down(3)


NAMES = ["x", "positions", "norm_mix", "norm_ffn", "lru_w_in", "lru_b_in", "lru_conv_w", "lru_conv_b", "lru_w_gate",
         "lru_b_gate", "lru_lambda", "lru_w_out", "lru_b_out", "kv_norm_in", "w_dkv", "kv_latent_norm", "w_ukv",
         "k_norm", "w_dq", "q_latent_norm", "w_uq", "q_norm", "w_o", "ffn_w_in", "ffn_w_out"]


def kernel(**inputs):
    import concourse.bacc as bacc
    from concourse.bass_utils import run_bass_kernel_spmd

    nc = bacc.Bacc("TRN2", target_bir_lowering=False, num_devices=1)
    arrays = {name: np.ascontiguousarray(inputs[name]) for name in NAMES}
    arrays["inv_freq"] = (10000.0 ** (-np.arange(0, ROPE, 2, dtype=np.float64) / ROPE)).astype(np.float32)[None, :]
    aps, feeds = {}, {}
    for name, arr in arrays.items():
        aps[name] = nc.dram_tensor(f"in_{name}", arr.shape, mybir.dt.from_np(arr.dtype), kind="ExternalInput").ap()
        feeds[f"in_{name}"] = arr
    out = nc.dram_tensor("out", (1, SEQ, D), F32, kind="ExternalOutput").ap()
    build_program(nc, aps, out)
    result = run_bass_kernel_spmd(nc, [feeds], core_ids=[0])
    return result.results[0]["out"]
```
